# Optimizing a Trainium2 kernel written in Bass

```python
import math
import jax, jax.numpy as jnp
from jax import lax
import numpy as np

D_MODEL = 1024
BATCH = 1
SEQ = 512
DEPTH = 2

CHUNK = 64
Q_BLOCK = 128
A_WIDTH = D_MODEL // 2
CONV_WIDTH = 31
B_WIDTH = D_MODEL // 2
LRU_BLOCKS = 8
LRU_BLOCK_DIM = B_WIDTH // LRU_BLOCKS
LRU_CONV_WIDTH = 4
LRU_C = 8.0
IN_WIDTH = 2 * A_WIDTH + 2 * B_WIDTH
DIFF_HEADS = D_MODEL // 128
DIFF_HEAD_DIM = 64
DIFF_V_DIM = 2 * DIFF_HEAD_DIM
QK_WIDTH = DIFF_HEADS * 2 * DIFF_HEAD_DIM
V_WIDTH = DIFF_HEADS * DIFF_V_DIM
ROPE_THETA = 10000.0
D_FF = ((8 * D_MODEL // 3 + 255) // 256) * 256
LN_EPS = 1e-5
DN_ALPHA = (2 * DEPTH) ** 0.25
DN_BETA = (8 * DEPTH) ** -0.25
N_EVEN = (DEPTH + 1) // 2
N_ODD = DEPTH // 2
NEG_INF = -1e30


def layer_norm(x, g, b):
    xf = x.astype(jnp.float32)
    mu = jnp.mean(xf, axis=-1, keepdims=True)
    var = jnp.mean(jnp.square(xf - mu), axis=-1, keepdims=True)
    return ((xf - mu) * lax.rsqrt(var + LN_EPS)).astype(x.dtype) * g + b

def rms_norm(x, g):
    xf = x.astype(jnp.float32)
    return (xf * lax.rsqrt(jnp.mean(jnp.square(xf), axis=-1, keepdims=True) + LN_EPS)).astype(x.dtype) * g

def causal_depthwise_conv(x, w, b):
    k, c = w.shape
    y = lax.conv_general_dilated(x, w[:, None, :].astype(x.dtype), window_strides=(1,),
                                 padding=[(k - 1, 0)], dimension_numbers=('NWC', 'WIO', 'NWC'),
                                 feature_group_count=c)
    return y + b

def _linear_recurrence_combine(c1, c2):
    a1, u1 = c1
    a2, u2 = c2
    return a1 * a2, a2 * u1 + u2

def rg_lru(x, w_a, b_a, w_x, b_x, lam):
    bsz, seq, width = x.shape
    xb = x.reshape(bsz, seq, LRU_BLOCKS, LRU_BLOCK_DIM)
    gate_r = jax.nn.sigmoid((jnp.einsum('bsgi,gij->bsgj', xb, w_a).reshape(bsz, seq, width) + b_a).astype(jnp.float32))
    gate_i = jax.nn.sigmoid((jnp.einsum('bsgi,gij->bsgj', xb, w_x).reshape(bsz, seq, width) + b_x).astype(jnp.float32))
    log_a = -LRU_C * gate_r * jax.nn.softplus(-lam.astype(jnp.float32))
    a = jnp.exp(log_a)
    u = jnp.sqrt(-jnp.expm1(2.0 * log_a)) * (gate_i * x.astype(jnp.float32))
    _, h = lax.associative_scan(_linear_recurrence_combine, (a, u), axis=1)
    return h.astype(x.dtype)

def conv_lru_mixer(x, w_in, b_in, conv_w, conv_b, cnorm_g, cnorm_b, lru_conv_w, lru_conv_b,
                   w_a, b_a, w_x, b_x, lru_lambda, w_out):
    h = x @ w_in + b_in
    a_val = h[..., :A_WIDTH]
    a_gate = h[..., A_WIDTH:2 * A_WIDTH]
    b_gate = h[..., 2 * A_WIDTH:2 * A_WIDTH + B_WIDTH]
    b_rec = h[..., 2 * A_WIDTH + B_WIDTH:]
    ya = jax.nn.silu(layer_norm(causal_depthwise_conv(a_val * jax.nn.sigmoid(a_gate), conv_w, conv_b),
                                cnorm_g, cnorm_b))
    yb = rg_lru(causal_depthwise_conv(b_rec, lru_conv_w, lru_conv_b), w_a, b_a, w_x, b_x, lru_lambda) \
        * jax.nn.gelu(b_gate)
    return jnp.concatenate([ya, yb], axis=-1) @ w_out

def rotate_half(t):
    half = t.shape[-1] // 2
    return jnp.concatenate([-t[..., half:], t[..., :half]], axis=-1)

def diff_attention_mixer(x, w_qkv, lq1, lk1, lq2, lk2, subln_g, w_out, lambda_init):
    bsz, seq, _ = x.shape
    qkv = x @ w_qkv
    q = qkv[..., :QK_WIDTH].reshape(bsz, seq, DIFF_HEADS, 2, DIFF_HEAD_DIM)
    k = qkv[..., QK_WIDTH:2 * QK_WIDTH].reshape(bsz, seq, DIFF_HEADS, 2, DIFF_HEAD_DIM)
    v = qkv[..., 2 * QK_WIDTH:].reshape(bsz, seq, DIFF_HEADS, DIFF_V_DIM)
    pos = jnp.arange(seq, dtype=jnp.float32)
    inv_freq = ROPE_THETA ** (-jnp.arange(0, DIFF_HEAD_DIM, 2, dtype=jnp.float32) / DIFF_HEAD_DIM)
    ang = pos[:, None] * inv_freq[None, :]
    ang = jnp.concatenate([ang, ang], axis=-1)
    cos = jnp.cos(ang).astype(x.dtype)[:, None, None, :]
    sin = jnp.sin(ang).astype(x.dtype)[:, None, None, :]
    q = (q * cos + rotate_half(q) * sin) * (DIFF_HEAD_DIM ** -0.5)
    k = k * cos + rotate_half(k) * sin
    q = q.transpose(0, 2, 3, 1, 4)
    k = k.transpose(0, 2, 3, 1, 4)
    v = v.transpose(0, 2, 1, 3)
    lam = (jnp.exp(jnp.sum(lq1.astype(jnp.float32) * lk1.astype(jnp.float32)))
           - jnp.exp(jnp.sum(lq2.astype(jnp.float32) * lk2.astype(jnp.float32))) + lambda_init)
    chunk_id = jnp.arange(seq) // CHUNK
    outs = []
    for qb in range(seq // Q_BLOCK):
        s0, s1 = qb * Q_BLOCK, (qb + 1) * Q_BLOCK
        scores = jnp.einsum('bhmqd,bhmkd->bhmqk', q[:, :, :, s0:s1], k[:, :, :, :s1],
                            preferred_element_type=jnp.float32)
        mask = chunk_id[s0:s1, None] >= chunk_id[None, :s1]
        p = jax.nn.softmax(jnp.where(mask, scores, NEG_INF), axis=-1)
        attn = p[:, :, 0] - lam * p[:, :, 1]
        outs.append(jnp.einsum('bhqk,bhkd->bhqd', attn.astype(v.dtype), v[:, :, :s1]))
    o = jnp.concatenate(outs, axis=2)
    o = rms_norm(o, subln_g) * (1.0 - lambda_init)
    o = o.transpose(0, 2, 1, 3).reshape(bsz, seq, V_WIDTH)
    return o @ w_out

def swiglu(x, w_gate, w_up, w_down):
    return (jax.nn.silu(x @ w_gate) * (x @ w_up)) @ w_down

def first_inputs(seed: int = 0) -> dict:
    key = jax.random.key(seed)
    ks = iter(jax.random.split(key, 40))
    f32 = jnp.float32

    def nrm(shape, scale):
        return scale * jax.random.normal(next(ks), shape, f32)

    def gain(shape):
        return 1.0 + nrm(shape, 0.02)

    a_pow = jax.random.uniform(next(ks), (N_EVEN, B_WIDTH), f32, minval=0.9, maxval=0.999)
    a0 = a_pow ** (1.0 / LRU_C)
    lru_lambda = jnp.log(a0) - jnp.log1p(-a0)
    return {
        'x': nrm((BATCH, SEQ, D_MODEL), 1.0),
        'even_w_in': nrm((N_EVEN, D_MODEL, IN_WIDTH), D_MODEL ** -0.5),
        'even_b_in': nrm((N_EVEN, IN_WIDTH), 0.01),
        'even_conv_w': nrm((N_EVEN, CONV_WIDTH, A_WIDTH), CONV_WIDTH ** -0.5),
        'even_conv_b': nrm((N_EVEN, A_WIDTH), 0.01),
        'even_cnorm_g': gain((N_EVEN, A_WIDTH)),
        'even_cnorm_b': nrm((N_EVEN, A_WIDTH), 0.01),
        'even_lru_conv_w': nrm((N_EVEN, LRU_CONV_WIDTH, B_WIDTH), LRU_CONV_WIDTH ** -0.5),
        'even_lru_conv_b': nrm((N_EVEN, B_WIDTH), 0.01),
        'even_w_a': nrm((N_EVEN, LRU_BLOCKS, LRU_BLOCK_DIM, LRU_BLOCK_DIM), LRU_BLOCK_DIM ** -0.5),
        'even_b_a': nrm((N_EVEN, B_WIDTH), 0.01),
        'even_w_x': nrm((N_EVEN, LRU_BLOCKS, LRU_BLOCK_DIM, LRU_BLOCK_DIM), LRU_BLOCK_DIM ** -0.5),
        'even_b_x': nrm((N_EVEN, B_WIDTH), 0.01),
        'even_lru_lambda': lru_lambda,
        'even_w_out': nrm((N_EVEN, A_WIDTH + B_WIDTH, D_MODEL), DN_BETA * (A_WIDTH + B_WIDTH) ** -0.5),
        'odd_w_qkv': nrm((N_ODD, D_MODEL, 2 * QK_WIDTH + V_WIDTH), D_MODEL ** -0.5),
        'odd_lambda_q1': nrm((N_ODD, DIFF_HEAD_DIM), 0.1),
        'odd_lambda_k1': nrm((N_ODD, DIFF_HEAD_DIM), 0.1),
        'odd_lambda_q2': nrm((N_ODD, DIFF_HEAD_DIM), 0.1),
        'odd_lambda_k2': nrm((N_ODD, DIFF_HEAD_DIM), 0.1),
        'odd_subln_g': gain((N_ODD, DIFF_V_DIM)),
        'odd_w_out': nrm((N_ODD, V_WIDTH, D_MODEL), DN_BETA * V_WIDTH ** -0.5),
        'mix_ln_g': gain((DEPTH, D_MODEL)),
        'mix_ln_b': nrm((DEPTH, D_MODEL), 0.01),
        'ffn_w_gate': nrm((DEPTH, D_MODEL, D_FF), D_MODEL ** -0.5),
        'ffn_w_up': nrm((DEPTH, D_MODEL, D_FF), D_MODEL ** -0.5),
        'ffn_w_down': nrm((DEPTH, D_FF, D_MODEL), DN_BETA * D_FF ** -0.5),
        'ffn_ln_g': gain((DEPTH, D_MODEL)),
        'ffn_ln_b': nrm((DEPTH, D_MODEL), 0.01),
    }

def first_block(x, even_w_in, even_b_in, even_conv_w, even_conv_b, even_cnorm_g, even_cnorm_b,
              even_lru_conv_w, even_lru_conv_b, even_w_a, even_b_a, even_w_x, even_b_x,
              even_lru_lambda, even_w_out, odd_w_qkv, odd_lambda_q1, odd_lambda_k1,
              odd_lambda_q2, odd_lambda_k2, odd_subln_g, odd_w_out, mix_ln_g, mix_ln_b,
              ffn_w_gate, ffn_w_up, ffn_w_down, ffn_ln_g, ffn_ln_b):
    for layer in range(DEPTH):
        if layer % 2 == 0:
            e = layer // 2
            y = conv_lru_mixer(x, even_w_in[e], even_b_in[e], even_conv_w[e], even_conv_b[e],
                               even_cnorm_g[e], even_cnorm_b[e], even_lru_conv_w[e], even_lru_conv_b[e],
                               even_w_a[e], even_b_a[e], even_w_x[e], even_b_x[e],
                               even_lru_lambda[e], even_w_out[e])
        else:
            o = layer // 2
            lambda_init = 0.8 - 0.6 * math.exp(-0.3 * layer)
            y = diff_attention_mixer(x, odd_w_qkv[o], odd_lambda_q1[o], odd_lambda_k1[o],
                                     odd_lambda_q2[o], odd_lambda_k2[o], odd_subln_g[o],
                                     odd_w_out[o], lambda_init)
        x = layer_norm(DN_ALPHA * x + y, mix_ln_g[layer], mix_ln_b[layer])
        x = layer_norm(DN_ALPHA * x + swiglu(x, ffn_w_gate[layer], ffn_w_up[layer], ffn_w_down[layer]),
                       ffn_ln_g[layer], ffn_ln_b[layer])
    return x


HEAD_DIM = 64
H_SB = 4
H_FOX = 4
H_MLA = 4
H_DIL = 4
N_HEADS_OUT = H_SB + H_FOX + H_MLA + H_DIL
D_MIX = N_HEADS_OUT * HEAD_DIM
MLA_Q_LORA = 256
MLA_KV_LORA = 128
MLA_NOPE = 64
MLA_ROPE = 32
MLA_V = HEAD_DIM
DIL_BRANCHES = ((128, 1), (512, 4), (2048, 16))
N_BR = len(DIL_BRANCHES)
N_SB = 3 * H_SB * HEAD_DIM
N_FOX = 3 * H_FOX * HEAD_DIM + H_FOX
N_MLA = MLA_Q_LORA + MLA_KV_LORA + MLA_ROPE
N_DIL = 3 * N_BR * H_DIL * HEAD_DIM
N_IN = N_SB + N_FOX + N_MLA + N_DIL
N_GROUPS = 4
EXPERTS_PER_GROUP = 4
N_EXPERTS = N_GROUPS * EXPERTS_PER_GROUP
TOP_K = 2
D_EXPERT = 512
MOE_BLOCK = 256
RMS_EPS = 1e-6


def _layernorm(x, g, b):
    xf = x.astype(jnp.float32)
    mu = jnp.mean(xf, -1, keepdims=True)
    var = jnp.mean(jnp.square(xf - mu), -1, keepdims=True)
    return ((xf - mu) * lax.rsqrt(var + LN_EPS) * g + b).astype(x.dtype)

def _rmsnorm(x, g):
    xf = x.astype(jnp.float32)
    return (xf * lax.rsqrt(jnp.mean(jnp.square(xf), -1, keepdims=True) + RMS_EPS) * g).astype(x.dtype)

def _rope(x, pos):
    half = x.shape[-1] // 2
    inv_freq = ROPE_THETA ** (-jnp.arange(half, dtype=jnp.float32) / half)
    ang = pos.astype(jnp.float32)[:, None] * inv_freq[None, :]
    cos = jnp.cos(ang)[None, :, None, :]
    sin = jnp.sin(ang)[None, :, None, :]
    xf = x.astype(jnp.float32)
    x1, x2 = xf[..., :half], xf[..., half:]
    return jnp.concatenate([x1 * cos - x2 * sin, x2 * cos + x1 * sin], -1).astype(x.dtype)

def _sweep(block_fn, seq):
    out = lax.map(block_fn, jnp.arange(seq // Q_BLOCK, dtype=jnp.int32) * Q_BLOCK)
    nb, b, h, blk, dv = out.shape
    return out.transpose(1, 2, 0, 3, 4).reshape(b, h, nb * blk, dv)

def _causal_softmax_sweep(logits_fn, v):
    seq = v.shape[2]
    kpos = jnp.arange(seq)

    def block(t0):
        logits = logits_fn(t0)
        qpos = t0 + jnp.arange(Q_BLOCK)
        mask = kpos[None, :] <= qpos[:, None]
        p = jax.nn.softmax(jnp.where(mask, logits, -jnp.inf), axis=-1)
        return jnp.einsum('bhqk,bhkd->bhqd', p.astype(v.dtype), v)

    return _sweep(block, seq)

def _stick_breaking_attention(q, k, v):
    seq = q.shape[2]
    scale = q.shape[-1] ** -0.5
    kpos = jnp.arange(seq)

    def block(t0):
        qb = lax.dynamic_slice_in_dim(q, t0, Q_BLOCK, axis=2)
        z = jnp.einsum('bhqd,bhkd->bhqk', qb, k).astype(jnp.float32) * scale
        qpos = t0 + jnp.arange(Q_BLOCK)
        before = kpos[None, :] < qpos[:, None]
        log_keep = jnp.where(before, jax.nn.log_sigmoid(-z), 0.0)
        log_after = lax.cumsum(log_keep, axis=3, reverse=True) - log_keep
        w = jnp.where(before, jnp.exp(jax.nn.log_sigmoid(z) + log_after), 0.0)
        return jnp.einsum('bhqk,bhkd->bhqd', w.astype(v.dtype), v)

    return _sweep(block, seq)

def _forgetting_attention(q, k, v, log_f):
    scale = q.shape[-1] ** -0.5
    c = jnp.cumsum(log_f, axis=-1)

    def logits(t0):
        qb = lax.dynamic_slice_in_dim(q, t0, Q_BLOCK, axis=2)
        cb = lax.dynamic_slice_in_dim(c, t0, Q_BLOCK, axis=2)
        s = jnp.einsum('bhqd,bhkd->bhqk', qb, k).astype(jnp.float32) * scale
        return s + cb[..., :, None] - c[..., None, :]

    return _causal_softmax_sweep(logits, v)

def _mla_attention(q_nope, q_rope, k_nope, k_rope, v):
    scale = (q_nope.shape[-1] + q_rope.shape[-1]) ** -0.5

    def logits(t0):
        qn = lax.dynamic_slice_in_dim(q_nope, t0, Q_BLOCK, axis=2)
        qr = lax.dynamic_slice_in_dim(q_rope, t0, Q_BLOCK, axis=2)
        s = (jnp.einsum('bhqd,bhkd->bhqk', qn, k_nope).astype(jnp.float32)
             + jnp.einsum('bhqr,bkr->bhqk', qr, k_rope).astype(jnp.float32))
        return s * scale

    return _causal_softmax_sweep(logits, v)

def _dilated_attention(qs, ks, vs):
    seq = qs[0].shape[1]
    scale = qs[0].shape[-1] ** -0.5

    def block(t0):
        qpos = t0 + jnp.arange(Q_BLOCK)
        outs, lses = [], []
        for (window, dil), q, k, v in zip(DIL_BRANCHES, qs, ks, vs):
            n_keys = window // dil + 1
            idx = qpos[:, None] - dil * jnp.arange(n_keys)[None, :]
            valid = idx >= 0
            idx = jnp.maximum(idx, 0)
            qb = lax.dynamic_slice_in_dim(q, t0, Q_BLOCK, axis=1)
            kb = jnp.take(k, idx, axis=1)
            vb = jnp.take(v, idx, axis=1)
            z = jnp.einsum('bqhd,bqnhd->bhqn', qb, kb).astype(jnp.float32) * scale
            z = jnp.where(valid[None, None], z, -jnp.inf)
            m = jnp.max(z, -1, keepdims=True)
            p = jnp.exp(z - m)
            den = jnp.sum(p, -1, keepdims=True)
            outs.append(jnp.einsum('bhqn,bqnhd->bhqd', (p / den).astype(v.dtype), vb).astype(jnp.float32))
            lses.append(m + jnp.log(den))
        mix = jax.nn.softmax(jnp.stack(lses), axis=0)
        return jnp.sum(mix * jnp.stack(outs), axis=0).astype(vs[0].dtype)

    return _sweep(block, seq)

def _mixing(x, w_in, b_forget, g_cq, g_ckv, w_uq, w_ukv, g_head, w_out):
    bsz, seq, _ = x.shape
    pos = jnp.arange(seq)
    proj = x @ w_in
    p_sb, p_fox, p_mla, p_dil = jnp.split(proj, [N_SB, N_SB + N_FOX, N_SB + N_FOX + N_MLA], axis=-1)

    def heads(t, n):
        return t.reshape(bsz, seq, n, -1).transpose(0, 2, 1, 3)

    q, k, v = jnp.split(p_sb, 3, axis=-1)
    o_sb = _stick_breaking_attention(heads(q, H_SB), heads(k, H_SB), heads(v, H_SB))

    hd = H_FOX * HEAD_DIM
    q, k, v, f = jnp.split(p_fox, [hd, 2 * hd, 3 * hd], axis=-1)
    log_f = jax.nn.log_sigmoid((f + b_forget).astype(jnp.float32)).transpose(0, 2, 1)
    o_fox = _forgetting_attention(heads(q, H_FOX), heads(k, H_FOX), heads(v, H_FOX), log_f)

    c_q, c_kv, k_r = jnp.split(p_mla, [MLA_Q_LORA, MLA_Q_LORA + MLA_KV_LORA], axis=-1)
    q = (_rmsnorm(c_q, g_cq) @ w_uq).reshape(bsz, seq, H_MLA, MLA_NOPE + MLA_ROPE)
    kv = (_rmsnorm(c_kv, g_ckv) @ w_ukv).reshape(bsz, seq, H_MLA, MLA_NOPE + MLA_V)
    q_rope = _rope(q[..., MLA_NOPE:], pos)
    k_rope = _rope(k_r[:, :, None, :], pos)[:, :, 0]
    tr = lambda a: a.transpose(0, 2, 1, 3)
    o_mla = _mla_attention(tr(q[..., :MLA_NOPE]), tr(q_rope), tr(kv[..., :MLA_NOPE]), k_rope,
                           tr(kv[..., MLA_NOPE:]))

    q, k, v = jnp.split(p_dil, 3, axis=-1)
    br = lambda a: a.reshape(bsz, seq, N_BR, H_DIL, HEAD_DIM)
    flat = lambda a: a.reshape(bsz, seq, N_BR * H_DIL, HEAD_DIM)
    q = br(_rope(flat(q), pos))
    k = br(_rope(flat(k), pos))
    v = br(v)
    o_dil = _dilated_attention([q[:, :, i] for i in range(N_BR)],
                               [k[:, :, i] for i in range(N_BR)],
                               [v[:, :, i] for i in range(N_BR)])

    o = jnp.concatenate([o_sb, o_fox, o_mla, o_dil], axis=1)
    o = _rmsnorm(o, g_head[None, :, None, :])
    return o.transpose(0, 2, 1, 3).reshape(bsz, seq, D_MIX) @ w_out

def _hier_moe(x, w_group, b_group, w_expert, b_expert, w1, w3, w2):
    n_tok, d = x.shape
    xf = x.astype(jnp.float32)
    g_logits = xf @ w_group.astype(jnp.float32) + b_group.astype(jnp.float32)
    g_sel = jnp.argmax(g_logits, axis=-1)
    g_w = jnp.take_along_axis(jax.nn.softmax(g_logits, -1), g_sel[:, None], axis=-1)
    e_logits = (xf @ w_expert.astype(jnp.float32) + b_expert.astype(jnp.float32)).reshape(
        n_tok, N_GROUPS, EXPERTS_PER_GROUP)
    e_in_group = jnp.take_along_axis(e_logits, g_sel[:, None, None], axis=1)[:, 0]
    top_logit, top_idx = lax.top_k(e_in_group, TOP_K)
    gate = jax.nn.softmax(top_logit, -1) * g_w
    expert_id = (g_sel[:, None] * EXPERTS_PER_GROUP + top_idx).reshape(-1).astype(jnp.int32)

    n_assign = n_tok * TOP_K
    n_slots = n_assign + N_EXPERTS * MOE_BLOCK
    n_chunks = n_slots // MOE_BLOCK
    tok_id = jnp.repeat(jnp.arange(n_tok, dtype=jnp.int32), TOP_K)
    order = jnp.argsort(expert_id)
    e_sorted = expert_id[order]
    counts = jnp.bincount(expert_id, length=N_EXPERTS)
    start = jnp.cumsum(counts) - counts
    padded = (counts + MOE_BLOCK - 1) // MOE_BLOCK * MOE_BLOCK
    pad_end = jnp.cumsum(padded)
    pad_start = pad_end - padded
    dest = pad_start[e_sorted] + jnp.arange(n_assign) - start[e_sorted]
    slot_tok = jnp.full((n_slots,), n_tok, jnp.int32).at[dest].set(tok_id[order])
    slot_gate = jnp.zeros((n_slots,), jnp.float32).at[dest].set(gate.reshape(-1)[order])
    chunk_expert = jnp.minimum(
        jnp.searchsorted(pad_end, jnp.arange(n_chunks) * MOE_BLOCK, side='right'), N_EXPERTS - 1)
    x_pad = jnp.concatenate([x, jnp.zeros((1, d), x.dtype)], axis=0)
    xs = x_pad[slot_tok].reshape(n_chunks, MOE_BLOCK, d)

    def expert_block(args):
        xb, e = args
        h = jax.nn.silu(xb @ w1[e]) * (xb @ w3[e])
        return h @ w2[e]

    ys = lax.map(expert_block, (xs, chunk_expert)).reshape(n_slots, d)
    ys = ys * slot_gate[:, None].astype(ys.dtype)
    return jax.ops.segment_sum(ys, slot_tok, num_segments=n_tok + 1)[:n_tok]

def second_inputs(seed: int = 0) -> dict:
    key = jax.random.key(seed)
    ks = jax.random.split(key, 20)
    L = DEPTH
    beta = (8.0 * DEPTH) ** -0.25
    f32 = jnp.float32

    def normal(k, shape, scale):
        return jax.random.normal(k, shape, f32) * scale

    return {
        'x': normal(ks[0], (BATCH, SEQ, D_MODEL), 1.0),
        'w_in': normal(ks[1], (L, D_MODEL, N_IN), D_MODEL ** -0.5),
        'b_forget': normal(ks[2], (L, H_FOX), 0.1),
        'g_cq': 1.0 + normal(ks[3], (L, MLA_Q_LORA), 0.02),
        'g_ckv': 1.0 + normal(ks[4], (L, MLA_KV_LORA), 0.02),
        'w_uq': normal(ks[5], (L, MLA_Q_LORA, H_MLA * (MLA_NOPE + MLA_ROPE)), MLA_Q_LORA ** -0.5),
        'w_ukv': normal(ks[6], (L, MLA_KV_LORA, H_MLA * (MLA_NOPE + MLA_V)), MLA_KV_LORA ** -0.5),
        'g_head': 1.0 + normal(ks[7], (L, N_HEADS_OUT, HEAD_DIM), 0.02),
        'w_out': normal(ks[8], (L, D_MIX, D_MODEL), beta * D_MIX ** -0.5),
        'ln1_g': 1.0 + normal(ks[9], (L, D_MODEL), 0.02),
        'ln1_b': normal(ks[10], (L, D_MODEL), 0.02),
        'w_group': normal(ks[11], (L, D_MODEL, N_GROUPS), D_MODEL ** -0.5),
        'b_group': normal(ks[12], (L, N_GROUPS), 0.01),
        'w_expert': normal(ks[13], (L, D_MODEL, N_EXPERTS), D_MODEL ** -0.5),
        'b_expert': normal(ks[14], (L, N_EXPERTS), 0.01),
        'w1': normal(ks[15], (L, N_EXPERTS, D_MODEL, D_EXPERT), D_MODEL ** -0.5),
        'w3': normal(ks[16], (L, N_EXPERTS, D_MODEL, D_EXPERT), D_MODEL ** -0.5),
        'w2': normal(ks[17], (L, N_EXPERTS, D_EXPERT, D_MODEL), beta * D_EXPERT ** -0.5),
        'ln2_g': 1.0 + normal(ks[18], (L, D_MODEL), 0.02),
        'ln2_b': normal(ks[19], (L, D_MODEL), 0.02),
    }

def second_block(x, w_in, b_forget, g_cq, g_ckv, w_uq, w_ukv, g_head, w_out, ln1_g, ln1_b,
              w_group, b_group, w_expert, b_expert, w1, w3, w2, ln2_g, ln2_b):
    alpha = (2.0 * DEPTH) ** 0.25
    bsz, seq, d = x.shape
    for l in range(DEPTH):
        h = _mixing(x, w_in[l], b_forget[l], g_cq[l], g_ckv[l], w_uq[l], w_ukv[l], g_head[l], w_out[l])
        x = _layernorm(alpha * x + h, ln1_g[l], ln1_b[l])
        m = _hier_moe(x.reshape(bsz * seq, d), w_group[l], b_group[l], w_expert[l], b_expert[l],
                      w1[l], w3[l], w2[l]).reshape(bsz, seq, d)
        x = _layernorm(alpha * x + m, ln2_g[l], ln2_b[l])
    return x


def setup_inputs(seed=0):
    out = dict(first_inputs(seed))
    for name, value in second_inputs(seed + 1).items():
        if name != "x":
            out[name + "_2"] = value
    return out


def reference(
    x, even_w_in, even_b_in, even_conv_w, even_conv_b, even_cnorm_g, even_cnorm_b,
    even_lru_conv_w, even_lru_conv_b, even_w_a, even_b_a, even_w_x, even_b_x, even_lru_lambda,
    even_w_out, odd_w_qkv, odd_lambda_q1, odd_lambda_k1, odd_lambda_q2, odd_lambda_k2,
    odd_subln_g, odd_w_out, mix_ln_g, mix_ln_b, ffn_w_gate, ffn_w_up, ffn_w_down, ffn_ln_g,
    ffn_ln_b, w_in_2, b_forget_2, g_cq_2, g_ckv_2, w_uq_2, w_ukv_2, g_head_2, w_out_2, ln1_g_2,
    ln1_b_2, w_group_2, b_group_2, w_expert_2, b_expert_2, w1_2, w3_2, w2_2, ln2_g_2, ln2_b_2,
):
    x = first_block(
        x, even_w_in, even_b_in, even_conv_w, even_conv_b, even_cnorm_g, even_cnorm_b,
        even_lru_conv_w, even_lru_conv_b, even_w_a, even_b_a, even_w_x, even_b_x,
        even_lru_lambda, even_w_out, odd_w_qkv, odd_lambda_q1, odd_lambda_k1, odd_lambda_q2,
        odd_lambda_k2, odd_subln_g, odd_w_out, mix_ln_g, mix_ln_b, ffn_w_gate, ffn_w_up,
        ffn_w_down, ffn_ln_g, ffn_ln_b,
    )
    return second_block(
        x, w_in_2, b_forget_2, g_cq_2, g_ckv_2, w_uq_2, w_ukv_2, g_head_2, w_out_2, ln1_g_2,
        ln1_b_2, w_group_2, b_group_2, w_expert_2, b_expert_2, w1_2, w3_2, w2_2, ln2_g_2,
        ln2_b_2,
    )


_drawn_inputs = setup_inputs


def setup_inputs(seed=0):
    import zlib

    import numpy as np

    out = dict(_drawn_inputs(seed))
    spreads = {}
    factors = {'even_b_in': 3.58,
     'even_conv_b': 4.077,
     'even_cnorm_g': 5.371,
     'even_cnorm_b': 6.999,
     'even_lru_conv_b': 3.647,
     'even_b_a': 42.303,
     'even_b_x': 33.098,
     'odd_subln_g': 5.683,
     'b_forget_2': 8.0,
     'g_cq_2': 8.0,
     'g_ckv_2': 5.064,
     'g_head_2': 3.994,
     'b_group_2': 23.966,
     'b_expert_2': 8.0}
    for name, (base, spread) in spreads.items():
        noise = np.random.default_rng([zlib.crc32(name.encode()), seed]).standard_normal(out[name].shape)
        drawn = base * np.exp(spread * noise) if base else spread * noise
        out[name] = __import__('jax').numpy.asarray(drawn.astype(out[name].dtype))
    for name, factor in factors.items():
        out[name] = (out[name] * factor).astype(out[name].dtype)
    return out
```

```python
from contextlib import ExitStack, contextmanager

import numpy as np

import concourse.bass as bass
from concourse import mybir

F32 = mybir.dt.float32
U32 = mybir.dt.uint32
ALU = mybir.AluOpType
ACT = mybir.ActivationFunctionType
AX = mybir.AxisListType

P = 128
T = 512
D = 1024
DT = D // P
QB = T // P
DEPTH = 2
FF = 2816
FT = FF // P
AT = 4
CONV = 31
LCONV = 4
HEADS1 = 8
ALPHA = (2 * DEPTH) ** 0.25
LAMBDA_INIT = 0.8 - 0.6 * float(np.exp(-0.3))
LN_EPS = 1e-5
RMS_EPS = 1e-6
NEG = -1e30
EXPERTS = 16
GROUPS = 4
ET = 4
RING = 4
SLOT = FT * P
BIG = 34
LAYERS2 = 2

DIL_Q, SB_Q, FOX_Q, CQ = 0, 6, 8, 10
DIL_K, SB_K, FOX_K = 12, 18, 20
DIL_V, SB_V, FOX_V = 22, 28, 30
CKV, MISC = 32, 33
W_IN2_GROUPS = 9
MLA_Q, MLA_KV, FOX_C = 0, 12, 22
HID, GATE = 0, 4
ROPE0, ROPE1 = 64, 96

M_BAND, M_TRI, M_MOD4, M_MOD16, M_CHUNK, M_STRICT, M_KEEP = 0, 128, 256, 768, 1280, 1408, 1536
M_COLS = 1664
C_ID, C_ONE, C_HALF, C_ROT, C_ROTM = 0, 128, 256, 384, 512
C_IOTA = 640
C_COLS = 656

PARAM1 = [("b_in", 16), ("conv_w", CONV * AT), ("conv_b", AT), ("cn_g", AT), ("cn_b", AT), ("lconv_w", LCONV * AT),
          ("lconv_b", AT), ("b_a", AT), ("b_x", AT), ("lam", AT), ("subln", 1), ("lamv", 256),
          ("mg0", DT), ("mb0", DT), ("fg0", DT), ("fb0", DT), ("mg1", DT), ("mb1", DT), ("fg1", DT), ("fb1", DT)]
PARAM2 = [("g_cq", 2), ("g_ckv", 1), ("g_head", DT), ("ln1_g", DT), ("ln1_b", DT), ("ln2_g", DT), ("ln2_b", DT),
          ("b_f", 1), ("router", DT * 20), ("router_b", 20)]


def columns(table):
    at, out = 0, {}
    for name, n in table:
        out[name] = at
        at += n
    return out, at


COL1, NP1 = columns(PARAM1)
COL2, NP2 = columns(PARAM2)


class Counts:

    def __init__(self, eng):
        self.eng, self.n, self.turns = eng, {}, []

    def of(self, event, scale=1, more=0):
        total = self.n.get(event, 0) * scale + more
        for reg, per in self.turns:
            if per.get(event):
                total = reg * (per[event] * scale) + total
        return total

    def add(self, event, k=1):
        self.n[event] = self.n.get(event, 0) + k

    @contextmanager
    def loop(self, turns, per):
        before = dict(self.n)
        with self.eng.Fori(0, turns) as i:
            self.turns.append((i, per))
            yield i
            self.turns.pop()
        for event in self.n:
            assert self.n[event] - before.get(event, 0) in (0, per.get(event, 0)), (event, self.n, before, per)
        self.n = {e: before.get(e, 0) + turns * per.get(e, 0) for e in {**self.n, **per}}


def steps_of(kind):
    plan = []
    for qb in range(QB):
        if kind == "dil":
            lo = max(qb - 1, 0)
            segs = [(0, 0, 64, lo, qb + 1 - lo, M_TRI + P - P * (qb + 1 - lo)),
                    (1, 0, 64, 0, qb + 1, M_MOD4 + T - P * (qb + 1)),
                    (2, 0, 64, 0, qb + 1, M_MOD16 + T - P * (qb + 1))]
        elif kind == "diff":
            segs = [(None, 64 * m, 64 * m + 64, 0, qb + 1, M_CHUNK) for m in range(2)]
        else:
            rows = {"sb": 64, "fox": 66, "mla": 96}[kind]
            segs = [(None, 0, rows, 0, qb + 1, None if kind == "sb" else M_TRI)]
        plan.append(segs)
    return plan


def blocks_of(kind, segs):
    if kind == "diff":
        return [(0, b) for b in range(segs[0][4])]
    return [(s, b) for s, seg in enumerate(segs) for b in range(seg[4])]


def t_turns(kind):
    values = 3 if kind == "dil" else 1
    return 2 * (values + sum(-(-len(blocks_of(kind, s)) // 4) for s in steps_of(kind)))


PAIR = {"steps": 2 * QB}
STAGED = {"dil": 9, "diff": 3, "sb": 3, "fox": 7, "mla": 4}


def build(nc, a, out):
    es = ExitStack()
    with es:
        def sb(name, *shape, dt=F32):
            return es.enter_context(nc.sbuf_tensor("sb_" + name, list(shape), dt))

        def sem(name):
            return es.enter_context(nc.semaphore(name))

        x = sb("x", P, DT, T)
        o = sb("o", P, DT, T)
        big = sb("big", P, BIG, T)
        shared = sb("shared", P, 10, T)
        ring = sb("ring", P, RING, SLOT)
        tabs = sb("tabs", P, 4, T)
        masks = sb("masks", P, M_COLS)
        consts = sb("consts", P, C_COLS)
        p1 = sb("p1", P, NP1)
        p2 = sb("p2", P, NP2)
        probs = sb("probs", P, 2, 1280)
        probs_t = sb("probs_t", P, 10, P)
        scan = sb("scan", P, T)
        vtok = sb("vtok", P, 1024)
        stat = sb("stat", P, 2, 16)
        small = sb("small", P, 40)
        route = sb("route", P, QB, 96)
        picks = sb("picks", P, QB, 8, dt=U32)
        sq = shared
        st_q, st_k, st_v = shared[:, 0:3, :], shared[:, 3:6, :], shared[:, 6:9, :]
        u_buf = o[:, :, :].rearrange("p a t -> p (a t)")[:, 0:AT * 544].rearrange("p (j t) -> p j t", t=544)
        rec = shared[:, :, :].rearrange("p a t -> p (a t)")[:, 0:AT * 520].rearrange("p (j t) -> p j t", t=520)
        gates_w = probs[:, :, :].rearrange("p a t -> p (a t)")[:, 0:1024].rearrange("p (j t) -> p j t", t=P)
        row = shared[:, 9, :]

        ident, ones = consts[:, C_ID:C_ID + P], consts[:, C_ONE:C_ONE + P]
        half1 = consts[:, C_HALF:C_HALF + P]
        ps = es.enter_context(nc.psum_tensor("ps", [P, 8, T], F32))

        w_full = [sem(f"w_full{b}") for b in range(RING)]
        tile_done = [sem(f"tile_done{b}") for b in range(RING)]
        bank_free = [sem(f"bank_free{b}") for b in range(RING)]
        phase_done = sem("phase_done")
        const_in = sem("const_in")
        settled = sem("settled")
        layer_in = sem("layer_in")
        gates_in = sem("gates_in")
        sg_ready = sem("sg_ready")
        norm_sum = sem("norm_sum")
        norm_dev = sem("norm_dev")
        norm_sq = sem("norm_sq")
        norm_var = sem("norm_var")
        norm_inv = sem("norm_inv")
        norm_rstd = sem("norm_rstd")
        norm_out = sem("norm_out")
        rot_full = [sem(f"rot_full{b}") for b in range(2)]
        rot_free = [sem(f"rot_free{b}") for b in range(2)]
        staged = [sem(f"staged{b}") for b in range(2)]
        scored = sem("scored")
        kept = sem("kept")
        max_ready = sem("max_ready")
        exp_done = sem("exp_done")
        p_ready = sem("p_ready")
        o_full = sem("o_full")
        o_free = sem("o_free")
        t_full = sem("t_full")
        t_free = sem("t_free")
        fox_rows = sem("fox_rows")
        kept_gate = sem("kept_gate")
        route_in = sem("route_in")
        route_exp = sem("route_exp")
        spread_in = sem("spread_in")
        spread_full = [sem(f"spread_full{b}") for b in range(2)]
        spread_free = [sem(f"spread_free{b}") for b in range(2)]
        out_done = sem("out_done")

        ENGINES = 3

        def settle(e):
            e.sem_inc(settled, 1)

        def phase_wait(e, c):
            e.wait_ge(phase_done, c.of("phase", ENGINES))
            settle(e)

        def phase(e, c):
            e.drain()
            e.sem_inc(phase_done, 1)
            c.add("phase")
            phase_wait(e, c)

        def load_tiles(e, c, groups, srcs, width):
            with c.loop(groups, {"group": 1}) as i:
                for b in range(RING):
                    e.wait_ge(tile_done[b], c.of("group", 1, 1))
                    src = srcs(i, b)
                    e.dma_start(ring[:, b, 0:width], src).then_inc(w_full[b], 16)
                c.add("group")

        def mul_tiles(e, c, groups, kt, rhs, rows=P):
            with c.loop(groups, {"group": 1}) as i:
                for b in range(RING):
                    e.wait_ge(w_full[b], c.of("group", 16, 16))
                    e.wait_ge(bank_free[b], c.of("group", 1, 1))
                    for k in range(kt):
                        m = e.matmul(ps[0:rows, b, :], ring[:, b, k * rows:(k + 1) * rows], rhs(k),
                                     start=k == 0, stop=k == kt - 1)
                    m.then_inc(tile_done[b], 1)
                c.add("group")

        def take_tiles(e, c, groups, take):
            with c.loop(groups, {"group": 1}) as i:
                for b in range(RING):
                    e.wait_ge(tile_done[b], c.of("group", 1, 2))
                    take(i, b).then_inc(bank_free[b], 1)
                c.add("group")

        def skip_tiles(c, groups):
            c.add("group", groups)

        def norm_pe(e, c, data, n, avg, centred=False, each=False):
            if centred:
                for j in range(n):
                    m = e.matmul(ps[:, 4, :], avg, data(j), start=j == 0, stop=j == n - 1)
                m.then_inc(norm_sum, 1)
            for j in range(n):
                e.wait_ge(norm_sq, c.of("norm_sq", 1, j + 1))
                if each and j >= 2:
                    e.wait_ge(norm_inv, c.of("norm_inv", 1, j - 1))
                m = e.matmul(ps[:, 5 + (j % 2 if each else 0), :], avg, sq[:, j, :],
                             start=each or j == 0, stop=each or j == n - 1)
                if each or j == n - 1:
                    m.then_inc(norm_var, 1)
            c.add("norm_sq", n)
            c.add("norm_inv", n if each else 1)

        def norm_dve(e, c, data, n, width, eps, centred=False, each=False, scaled=None):
            if centred:
                e.wait_ge(norm_sum, c.of("norm_sum", 1, 1))
                c.add("norm_sum")
                for j in range(n):
                    e.scalar_tensor_tensor(data(j), ps[:, 4, :], -1.0 / width, data(j), ALU.mult,
                                           ALU.add).then_inc(norm_dev, 1)
            for g in range(n if each else 1):
                e.wait_ge(norm_var, c.of("norm_var", 1, 1))
                if g:
                    settle(e)
                    e.drain()
                e.tensor_scalar(row, ps[:, 5 + g % 2, :], 1.0 / width, eps, ALU.mult, ALU.add)
                e.drain()
                e.reciprocal(row, row).then_inc(norm_inv, 1)
                e.wait_ge(norm_rstd, c.of("norm_rstd", 1, 1))
                c.add("norm_var")
                c.add("norm_rstd")
                for j in [g] if each else range(n):
                    if scaled:
                        e.scalar_tensor_tensor(data(j), data(j), scaled(j), row, ALU.mult, ALU.mult)
                    else:
                        e.tensor_tensor(data(j), data(j), row, ALU.mult).then_inc(norm_out, 1)

        def norm_act(e, c, data, n, centred=False, each=False, final=None):
            for j in range(n):
                if centred:
                    e.wait_ge(norm_dev, c.of("norm_dev", 1, j + 1))
                e.activation(sq[:, j, :], data(j), ACT.Square).then_inc(norm_sq, 1)
            if centred:
                c.add("norm_dev", n)
            for _ in range(n if each else 1):
                e.wait_ge(norm_inv, c.of("norm_inv", 1, 1))
                c.add("norm_inv")
                e.activation(row, row, ACT.Sqrt).then_inc(norm_rstd, 1)
            if final:
                for j in range(n):
                    e.wait_ge(norm_out, c.of("norm_out", 1, j + 1))
                    final(e, j)
                c.add("norm_out", n)

        def x_tile(j):
            return x[:, j, :]

        def o_tile(j):
            return o[:, j, :]

        def affine(params, gain, shift):
            def final(e, j, src):
                e.activation(x[:, j, :], src(j), ACT.Identity, bias=params[:, shift + j:shift + j + 1],
                             scale=params[:, gain + j:gain + j + 1])
            return final

        def rope_pe(e, c, pairs, rot, tile):
            with c.loop(pairs, {"rope": 1}) as i:
                for b in range(2):
                    e.wait_ge(rot_free[b], c.of("rope", 1, 1))
                    e.matmul(ps[:, b, :], rot, big[:, tile(i, b), :], start=True, stop=True).then_inc(rot_full[b], 1)
                c.add("rope")

        def rope_dve(e, c, pairs, cos, sin, tile):
            with c.loop(pairs, {"rope": 1}) as i:
                for b in range(2):
                    e.wait_ge(rot_full[b], c.of("rope", 1, 1))
                    e.tensor_tensor(probs[:, b, 0:T], ps[:, b, :], sin, ALU.mult).then_inc(rot_free[b], 1)
                    e.tensor_tensor(big[:, tile(i, b), :], big[:, tile(i, b), :], cos, ALU.mult)
                e.drain()
                for b in range(2):
                    e.tensor_tensor(big[:, tile(i, b), :], big[:, tile(i, b), :], probs[:, b, 0:T], ALU.add)
                e.drain()
                c.add("rope")

        LEAD = 8
        SETS = 2

        def order(kind):
            alone = kind == "dil"
            for t in range(2 * QB):
                if t % QB == 0:
                    if alone and t:
                        yield "tail", t - 1
                    yield "values", t // QB
                yield "head", t
                if t and not (alone and t % QB == 0):
                    yield "tail", t - 1
            yield "tail", 2 * QB - 1

        def per_turn(kind):
            return {"steps": 2 * QB, "turns": t_turns(kind), "st0": STAGED[kind], "st1": STAGED[kind],
                    "kept": 2 * QB if kind == "sb" else 0}

        def width_of(kind):
            return P if kind == "diff" else 64

        def bank(t, s):
            return 3 * (t % 2) + s

        def offsets(segs):
            return [sum(P * g[4] for g in segs[:s]) for s in range(len(segs))]

        def v_at(kind, slot, kb):
            w = width_of(kind)
            return vtok[:, (slot * QB + kb) * w:(slot * QB + kb + 1) * w]

        def attend_sp(e, c, kind, pairs):
            with c.loop(pairs, per_turn(kind)) as i:
                for a in range(2):
                    e.wait_ge(scored, c.of("steps", 1, QB * a + (LEAD if kind == "dil" else QB)))
                    h = slice(64 * a, 64 * a + 64)
                    moves = []
                    if kind == "dil":
                        for br in range(3):
                            moves += [(st_q[0:64, br, :], big[h, i + (DIL_Q + 2 * br), :]),
                                      (st_k[0:64, br, :], big[h, i + (DIL_K + 2 * br), :]),
                                      (st_v[0:64, br, :], big[h, i + (DIL_V + 2 * br), :])]
                    elif kind == "diff":
                        moves = [(st_q[:, a, :], big[:, i * 2 + a, :]),
                                 (st_k[:, a, :], big[:, i * 2 + (HEADS1 + a), :]),
                                 (st_v[:, a, :], big[:, i * 2 + (2 * HEADS1 + a), :])]
                    elif kind == "mla":
                        moves = [(st_q[0:96, a, :], big[0:96, i * 2 + (MLA_Q + a), :]),
                                 (st_k[0:64, a, :], big[0:64, i * 2 + (MLA_KV + a), :]),
                                 (st_k[ROPE0:ROPE1, a, :], big[ROPE0:ROPE1, MISC, :]),
                                 (st_v[0:64, a, :], big[64:P, i * 2 + (MLA_KV + a), :])]
                    else:
                        q, k, v = (SB_Q, SB_K, SB_V) if kind == "sb" else (FOX_Q, FOX_K, FOX_V)
                        moves = [(st_q[0:64, a, :], big[h, i + q, :]), (st_k[0:64, a, :], big[h, i + k, :]),
                                 (st_v[0:64, a, :], big[h, i + v, :])]
                        if kind == "fox":
                            moves += [(st_q[64:65, a, :], big[0:1, i * 2 + (FOX_C + a), :]),
                                      (st_q[65:66, a, :], big[64:65, FOX_C, :]),
                                      (st_k[64:65, a, :], big[64:65, FOX_C, :]),
                                      (st_k[65:66, a, :], big[32:33, i * 2 + (FOX_C + a), :])]
                    assert len(moves) == STAGED[kind]
                    for dst, src in moves:
                        e.dma_start(dst, src).then_inc(staged[a], 16)
                c.add("steps", 2 * QB)
                c.add("turns", t_turns(kind))
                c.add("st0", STAGED[kind])
                c.add("st1", STAGED[kind])
                c.add("kept", 2 * QB if kind == "sb" else 0)

        def attend_pe(e, c, kind, pairs):
            plan, w = steps_of(kind), width_of(kind)
            with c.loop(pairs, per_turn(kind)) as i:
                for what, t in order(kind):
                    if what == "values":
                        a = t
                        e.wait_ge(staged[a], c.of(f"st{a}", 16, 16 * STAGED[kind]))
                        c.add(f"st{a}", STAGED[kind])
                        for slot in range(3) if kind == "dil" else [a]:
                            e.wait_ge(t_free, c.of("turns", 1, 1))
                            settle(e)
                            for kb in range(QB):
                                m = e.transpose(ps[:, 6, kb * w:(kb + 1) * w], st_v[0:w, slot, kb * P:(kb + 1) * P],
                                                ident[0:w, 0:w])
                            m.then_inc(t_full, 1)
                            c.add("turns")
                    elif what == "head":
                        e.wait_ge(exp_done, c.of("steps", 1, t + 1))
                        segs = plan[t % QB]
                        for s, (slot, r0, r1, kb, n, _) in enumerate(segs):
                            slot = t // QB if slot is None else slot
                            m = e.matmul(ps[:, bank(t, s), 0:n * P], st_q[r0:r1, slot, (t % QB) * P:(t % QB + 1) * P],
                                         st_k[r0:r1, slot, kb * P:(kb + n) * P], start=True, stop=True)
                        m.then_inc(scored, 1)
                    else:
                        segs = plan[t % QB]
                        at, blocks = offsets(segs), blocks_of(kind, segs)
                        e.wait_ge(p_ready, c.of("steps", 1, t + 1))
                        for g in range(0, len(blocks), 4):
                            e.wait_ge(t_free, c.of("turns", 1, 1))
                            for j, (s, b) in enumerate(blocks[g:g + 4]):
                                m = e.transpose(ps[:, 6, j * P:(j + 1) * P],
                                                probs[:, t % 2, at[s] + b * P:at[s] + (b + 1) * P], ident)
                            m.then_inc(t_full, 1)
                            c.add("turns")
                        e.wait_ge(t_free, c.of("turns", 1, 1))
                        e.wait_ge(o_free, c.of("steps", 1, t + 1))
                        for j, (s, b) in enumerate(blocks):
                            slot = t // QB if segs[s][0] is None else segs[s][0]
                            m = e.matmul(ps[0:w, 7, 0:P], v_at(kind, slot, segs[s][3] + b), probs_t[:, j, :],
                                         start=j == 0, stop=j == len(blocks) - 1)
                        m.then_inc(o_full, 1)
                c.add("steps", 2 * QB)
                c.add("kept", 2 * QB if kind == "sb" else 0)

        def attend_act(e, c, kind, pairs):
            plan, w = steps_of(kind), width_of(kind)
            with c.loop(pairs, per_turn(kind)) as i:
                for what, t in order(kind):
                    if what == "values":
                        e.wait_ge(o_full, c.of("steps", 1, SETS + (QB * t if kind == "dil" else 0)))
                        for slot in range(3) if kind == "dil" else [t]:
                            e.wait_ge(t_full, c.of("turns", 1, 1))
                            e.copy(vtok[:, slot * QB * w:(slot + 1) * QB * w], ps[:, 6, 0:QB * w]).then_inc(t_free, 1)
                            c.add("turns")
                    elif what == "head":
                        segs = plan[t % QB]
                        at = offsets(segs)
                        e.wait_ge(o_full, c.of("steps", 1, t + 1))
                        if kind == "sb":
                            n = segs[0][4] * P
                            z, p = ps[:, bank(t, 0), 0:n], probs[:, t % 2, 0:n]
                            e.wait_ge(scored, c.of("steps", 1, LEAD + t + 1))
                            e.activation(p, z, ACT.Abs)
                            e.drain()
                            e.activation(p, p, ACT.Exp, scale=-1.0)
                            e.drain()
                            e.activation(p, p, ACT.Ln, bias=1.0).then_inc(kept, 1)
                            e.wait_ge(max_ready, c.of("steps", 1, t + 1))
                            e.activation(p, p, ACT.Exp).then_inc(exp_done, 1)
                        else:
                            e.wait_ge(max_ready, c.of("steps", 1, t + 1))
                            for s, seg in enumerate(segs):
                                bias = s if kind == "diff" else 0
                                m = e.activation(probs[:, t % 2, at[s]:at[s] + seg[4] * P],
                                                 ps[:, bank(t, s), 0:seg[4] * P], ACT.Exp,
                                                 bias=stat[:, t % 2, bias:bias + 1],
                                                 accum_out=stat[:, t % 2, 8 + s:9 + s])
                            m.then_inc(exp_done, 1)
                    else:
                        e.wait_ge(o_full, c.of("steps", 1, SETS + t))
                        n = len(blocks_of(kind, plan[t % QB]))
                        for g in range(0, n, 4):
                            k = min(4, n - g)
                            e.wait_ge(t_full, c.of("turns", 1, 1))
                            e.copy(probs_t[:, g:g + k, :].rearrange("p a t -> p (a t)"), ps[:, 6, 0:k * P])\
                                .then_inc(t_free, 1)
                            c.add("turns")
                c.add("steps", 2 * QB)
                c.add("st0", STAGED[kind])
                c.add("st1", STAGED[kind])
                c.add("kept", 2 * QB if kind == "sb" else 0)

        def attend_dve(e, c, kind, pairs, o_first):
            plan, w = steps_of(kind), width_of(kind)

            def take_output(i, t):
                a, qs = t // QB, slice((t % QB) * P, (t % QB + 1) * P)
                dst = o[:, i * 2 + a, qs] if kind == "diff" else o[64 * a:64 * a + 64, i + o_first, qs]
                e.wait_ge(o_full, c.of("steps", 1, SETS + t + 1))
                e.tensor_copy(dst, ps[0:w, 7, 0:P]).then_inc(o_free, 1)

            with c.loop(pairs, per_turn(kind)) as i:
                for what, t in order(kind):
                    if what == "values":
                        continue
                    segs = plan[t % QB]
                    at = offsets(segs)
                    st = stat[:, t % 2, :]
                    if what == "head" and kind == "sb":
                        n = segs[0][4] * P
                        z, p = ps[:, bank(t, 0), 0:n], probs[:, t % 2, 0:n]
                        e.wait_ge(kept, c.of("kept", 1, t + 1))
                        e.scalar_tensor_tensor(p, z, 0.0, p, ALU.max, ALU.add)
                        e.drain()
                        e.tensor_tensor(p[:, n - P:n], p[:, n - P:n], masks[:, M_KEEP:M_KEEP + P], ALU.mult)
                        e.drain()
                        e.tensor_tensor_scan(scan[:, 0:n][:, ::-1], p[:, ::-1], p[:, ::-1], 0.0, ALU.add, ALU.bypass)
                        e.drain()
                        e.tensor_tensor(p, z, scan[:, 0:n], ALU.subtract)
                        e.drain()
                        e.tensor_tensor(p[:, n - P:n], p[:, n - P:n], masks[:, M_STRICT:M_STRICT + P], ALU.add)\
                            .then_inc(max_ready, 1)
                    elif what == "head":
                        e.wait_ge(scored, c.of("steps", 1, LEAD + t + 1))
                        for s, seg in enumerate(segs):
                            n = seg[4] * P
                            m0 = 0 if kind == "dil" else n - P
                            z = ps[:, bank(t, s), m0:n]
                            e.tensor_tensor(z, z, masks[:, seg[5]:seg[5] + n - m0], ALU.add)
                        e.drain()
                        for s, seg in enumerate(segs):
                            col = 4 + s if kind == "dil" else s
                            m = e.tensor_reduce(st[:, col:col + 1], ps[:, bank(t, s), 0:seg[4] * P], AX.X, ALU.max,
                                                negate=kind != "dil")
                        if kind == "dil":
                            e.drain()
                            m = e.tensor_reduce(st[:, 0:1], st[:, 4:7], AX.X, ALU.max, negate=True)
                        m.then_inc(max_ready, 1)
                    else:
                        e.wait_ge(exp_done, c.of("steps", 1, SETS + t + 1))
                        if kind == "sb":
                            e.sem_inc(p_ready, 1)
                        elif kind == "diff":
                            n = segs[0][4] * P
                            p0, p1_ = probs[:, t % 2, 0:n], probs[:, t % 2, n:2 * n]
                            e.reciprocal(st[:, 12:14], st[:, 8:10])
                            e.drain()
                            e.tensor_scalar(p1_, p1_, st[:, 13:14], small[:, 4:5], ALU.mult, ALU.mult)
                            e.drain()
                            e.scalar_tensor_tensor(p0, p0, st[:, 12:13], p1_, ALU.mult, ALU.add).then_inc(p_ready, 1)
                        else:
                            n = sum(seg[4] for seg in segs) * P
                            if kind == "dil":
                                e.tensor_reduce(st[:, 11:12], st[:, 8:11], AX.X, ALU.add)
                                e.drain()
                            total = 11 if kind == "dil" else 8
                            e.reciprocal(st[:, 12:13], st[:, total:total + 1])
                            e.drain()
                            e.tensor_scalar(probs[:, t % 2, 0:n], probs[:, t % 2, 0:n], st[:, 12:13], None, ALU.mult)\
                                .then_inc(p_ready, 1)
                        if t:
                            take_output(i, t - 1)
                take_output(i, 2 * QB - 1)
                c.add("steps", 2 * QB)
                c.add("turns", t_turns(kind))
                c.add("st0", STAGED[kind])
                c.add("st1", STAGED[kind])
                c.add("kept", 2 * QB if kind == "sb" else 0)

        RG, RE, RPAD, RMAX, RIDX, RSEL, RV, RW = 0, 4, 24, 32, 40, 44, 48, 64

        def route_dve(e, c):
            iota = consts[:, C_IOTA:C_IOTA + EXPERTS]
            e.memset(route[:, :, RPAD:RPAD + 8], NEG)
            for q in range(QB):
                e.tensor_tensor(route[:, q, 0:20], ps[:, 0, 20 * q:20 * q + 20],
                                p2[:, COL2["router_b"]:COL2["router_b"] + 20], ALU.add)
            e.drain()
            e.tensor_copy(route[:, :, RPAD:RPAD + GROUPS], route[:, :, RG:RG + GROUPS])
            e.drain()
            for q in range(QB):
                e.max(route[:, q, RMAX:RMAX + 8], route[:, q, RPAD:RPAD + 8])
            e.drain()
            for q in range(QB):
                e.max_index(picks[:, q, :], route[:, q, RMAX:RMAX + 8], route[:, q, RPAD:RPAD + 8])
            for q in range(QB):
                e.tensor_scalar(route[:, q, RV:RV + GROUPS], route[:, q, RG:RG + GROUPS],
                                route[:, q, RMAX:RMAX + 1], None, ALU.subtract)
            e.drain()
            e.tensor_copy(route[:, :, RIDX:RIDX + 1], picks[:, :, 0:1]).then_inc(route_in, 1)
            e.drain()
            for q in range(QB):
                e.tensor_scalar(route[:, q, RSEL:RSEL + GROUPS], iota[:, 0:GROUPS], route[:, q, RIDX:RIDX + 1], None,
                                ALU.is_equal)
            e.drain()
            e.tensor_scalar(route[:, :, RSEL:RSEL + GROUPS], route[:, :, RSEL:RSEL + GROUPS], 1.0, -NEG,
                            ALU.subtract, ALU.mult)
            e.drain()
            for j in range(EXPERTS // GROUPS):
                view = route[:, :, RE + j:RE + EXPERTS:GROUPS]
                e.tensor_tensor(view, view, route[:, :, RSEL:RSEL + GROUPS], ALU.add)
            e.drain()
            for q in range(QB):
                e.max(route[:, q, RMAX:RMAX + 8], route[:, q, RE:RE + EXPERTS])
            e.drain()
            for q in range(QB):
                e.max_index(picks[:, q, :], route[:, q, RMAX:RMAX + 8], route[:, q, RE:RE + EXPERTS])
            e.tensor_tensor(route[:, :, RW:RW + 1], route[:, :, RMAX + 1:RMAX + 2], route[:, :, RMAX:RMAX + 1],
                            ALU.subtract).then_inc(route_in, 1)
            e.drain()
            e.tensor_copy(route[:, :, RIDX:RIDX + 2], picks[:, :, 0:2])
            e.wait_ge(route_exp, c.of("routes", 2, 2))
            c.add("routes")
            for q in range(QB):
                e.tensor_reduce(route[:, q, RW + 2:RW + 3], route[:, q, RV:RV + GROUPS], AX.X, ALU.add)
            e.tensor_scalar(route[:, :, RW + 3:RW + 4], route[:, :, RW:RW + 1], 1.0, None, ALU.add)
            e.drain()
            e.tensor_tensor(route[:, :, RW + 4:RW + 5], route[:, :, RW + 2:RW + 3], route[:, :, RW + 3:RW + 4], ALU.mult)
            e.drain()
            e.reciprocal(route[:, :, RW + 5:RW + 6], route[:, :, RW + 4:RW + 5])
            e.drain()
            e.tensor_tensor(route[:, :, RW + 6:RW + 7], route[:, :, RW + 5:RW + 6], route[:, :, RW:RW + 1], ALU.mult)
            e.drain()
            for q in range(QB):
                e.tensor_scalar(route[:, q, RE:RE + EXPERTS], iota, route[:, q, RIDX:RIDX + 1],
                                route[:, q, RW + 5:RW + 6], ALU.is_equal, ALU.mult)
                e.tensor_scalar(route[:, q, 72:72 + EXPERTS], iota, route[:, q, RIDX + 1:RIDX + 2],
                                route[:, q, RW + 6:RW + 7], ALU.is_equal, ALU.mult)
            e.drain()
            e.tensor_tensor(route[:, :, RE:RE + EXPERTS], route[:, :, RE:RE + EXPERTS], route[:, :, 72:72 + EXPERTS],
                            ALU.add)
            for j in range(DT):
                e.tensor_scalar(o[:, j, :], x[:, j, :], ALPHA, None, ALU.mult)
            e.drain()
            for k in range(EXPERTS):
                if k >= 2:
                    e.wait_ge(spread_full[k % 2], c.of("spread", 1, k // 2))
                for q in range(QB):
                    m = e.tensor_scalar(probs[:, k % 2, q * P:(q + 1) * P], ones, route[:, q, RE + k:RE + k + 1], None,
                                        ALU.mult)
                m.then_inc(spread_in, 1)
            c.add("spread", EXPERTS // 2)

        def route_act(e, c):
            e.wait_ge(route_in, c.of("routes", 2, 1))
            e.activation(route[:, :, RV:RV + GROUPS], route[:, :, RV:RV + GROUPS], ACT.Exp).then_inc(route_exp, 1)
            e.wait_ge(route_in, c.of("routes", 2, 2))
            e.activation(route[:, :, RW:RW + 1], route[:, :, RW:RW + 1], ACT.Exp).then_inc(route_exp, 1)
            c.add("routes")

        def route_pe(e):
            for q in range(QB):
                for k in range(DT):
                    e.matmul(ps[:, 0, 20 * q:20 * q + 20], x[:, k, q * P:(q + 1) * P],
                             p2[:, COL2["router"] + 20 * k:COL2["router"] + 20 * k + 20], start=k == 0, stop=k == DT - 1)

        def spread_pe(e, c):
            for k in range(EXPERTS):
                e.wait_ge(spread_in, c.of("spread", 2, k + 1))
                e.wait_ge(spread_free[k % 2], c.of("spread", 1, k // 2 + 1))
                for q in range(QB):
                    m = e.matmul(ps[:, 1 + k % 2, q * P:(q + 1) * P], probs[:, k % 2, q * P:(q + 1) * P], ident,
                                 start=True, stop=True)
                m.then_inc(spread_full[k % 2], 1)
            c.add("spread", EXPERTS // 2)

        def spread_act(e, c):
            for k in range(EXPERTS):
                e.wait_ge(spread_full[k % 2], c.of("spread", 1, k // 2 + 1))
                e.copy(big[:, GATE + k, :], ps[:, 1 + k % 2, :]).then_inc(spread_free[k % 2], 1)
            c.add("spread", EXPERTS // 2)

        block = es.enter_context(nc.Block())
        LAYER = {"group": W_IN2_GROUPS + 2 + 2 + 4 * EXPERTS, "phase": 14, "layer": 1, "rope": 6 + 3, "steps": 2 * 8 * 4,
                 "routes": 1, "spread": EXPERTS // 2, "norm_sum": 2, "norm_dev": 2 * DT, "norm_out": 2 * DT,
                 "norm_sq": 3 * DT + 3, "norm_inv": 4 + DT, "norm_var": 4 + DT, "norm_rstd": 4 + DT, "fox": 1,
                 "kept": 16, "turns": 2 * sum(t_turns(k) for k in ("dil", "mla", "fox", "sb")),
                 "st0": 2 * sum(STAGED[k] for k in ("dil", "mla", "fox", "sb")),
                 "st1": 2 * sum(STAGED[k] for k in ("dil", "mla", "fox", "sb"))}

        @block.sync
        def _(e):
            c = Counts(e)

            def load(dst, src, s):
                e.dma_start(dst, src).then_inc(s, 16)

            def feed_forward(layer):
                load_tiles(e, c, FT // 2, lambda i, b: a["w_up" if b % 2 else "w_gate"][layer, i * 2 + b // 2], DT * P)
                load_tiles(e, c, 2, lambda i, b: a["w_down"][layer, i * RING + b], FT * P)

            load(x[:, :, :], a["x"], const_in)
            load(p1[:, :], a["p1"], const_in)
            load(consts[:, :], a["consts"], const_in)
            load(masks[:, :], a["masks"], const_in)
            load(tabs[:, :, :], a["tabs"], const_in)
            load(gates_w, a["gates"], const_in)
            load_tiles(e, c, 4, lambda i, b: a["w_in"][i * RING + b], DT * P)
            load_tiles(e, c, 2, lambda i, b: a["w_out"][i * RING + b], DT * P)
            feed_forward(0)
            c.add("phase", 9)
            load_tiles(e, c, 6, lambda i, b: a["w_qkv"][i * RING + b], DT * P)
            c.add("phase", 2)
            phase_wait(e, c)
            attend_sp(e, c, "diff", HEADS1 // 2)
            load_tiles(e, c, 2, lambda i, b: a["w_out1"][i * RING + b], DT * P)
            feed_forward(1)
            c.add("phase", 7)
            with c.loop(LAYERS2, LAYER) as l:
                phase_wait(e, c)
                load(p2[:, :], a["p2"][l], layer_in)
                load_tiles(e, c, W_IN2_GROUPS, lambda i, b: a["w_in2"][l, i * RING + b], DT * P)
                c.add("phase", 2)
                phase_wait(e, c)
                attend_sp(e, c, "dil", 2)
                load_tiles(e, c, 1, lambda i, b: a["w_uq"][l, b], 2 * ROPE1)
                load_tiles(e, c, 1, lambda i, b: a["w_ukv"][l, b], P)
                c.add("phase", 2)
                phase_wait(e, c)
                for h in range(4):
                    load(big[0:1, FOX_C + h, :], probs[h:h + 1, 0, T:2 * T], fox_rows)
                    load(big[32:33, FOX_C + h, :], probs[h:h + 1, 1, T:2 * T], fox_rows)
                e.wait_ge(fox_rows, c.of("fox", 8 * 16, 8 * 16))
                settle(e)
                c.add("fox")
                c.add("phase", 2)
                phase_wait(e, c)
                attend_sp(e, c, "mla", 2)
                attend_sp(e, c, "fox", 2)
                attend_sp(e, c, "sb", 2)
                load_tiles(e, c, 2, lambda i, b: a["w_out2"][l, i * RING + b], DT * P)
                with c.loop(EXPERTS, {"group": 4}) as k:
                    for half in range(2):
                        for b in range(RING):
                            e.wait_ge(tile_done[b], c.of("group", 1, 1))
                            e.dma_start(ring[:, b, 0:DT * P], a["w3" if b % 2 else "w1"][l, k, 2 * half + b // 2])\
                                .then_inc(w_full[b], 16)
                        c.add("group")
                    for half in range(2):
                        for b in range(RING):
                            e.wait_ge(tile_done[b], c.of("group", 1, 1))
                            e.dma_start(ring[:, b, 0:ET * P], a["w2"][l, k, RING * half + b]).then_inc(w_full[b], 16)
                        c.add("group")
                c.add("phase", 8)
            phase_wait(e, c)
            load(out, x[:, :, :], out_done)
            e.wait_ge(out_done, 16)

        @block.tensor
        def _(e):
            c = Counts(e)
            e.sem_inc(scored, LEAD)
            for s in (*tile_done, *bank_free, *rot_free, *spread_free, t_free, o_free):
                e.sem_inc(s, 1)
            e.sem_inc(o_full, SETS)

            def ln(data):
                norm_pe(e, c, data, DT, ones, centred=True)
                phase(e, c)

            def feed_forward():
                mul_tiles(e, c, FT // 2, DT, x_tile)
                phase(e, c)
                mul_tiles(e, c, 2, FT, lambda k: big[:, k, :])
                phase(e, c)
                ln(x_tile)

            e.wait_ge(const_in, 6 * 16)
            mul_tiles(e, c, 4, DT, x_tile)
            phase(e, c)
            phase(e, c)
            for j in range(AT):
                for g in range(2):
                    m = e.matmul(ps[:, 4 * g + j, :], gates_w[:, AT * g + j, :], big[:, 12 + j, :], start=True, stop=True)
                m.then_inc(sg_ready, 1)
            phase(e, c)
            norm_pe(e, c, lambda j: big[:, 8 + j, :], AT, ones, centred=True)
            phase(e, c)
            mul_tiles(e, c, 2, DT, lambda k: big[:, 8 + k, :])
            phase(e, c)
            ln(x_tile)
            feed_forward()
            mul_tiles(e, c, 6, DT, x_tile)
            phase(e, c)
            rope_pe(e, c, HEADS1, consts[:, C_ROT:C_ROT + P], lambda i, b: i * 2 + b)
            phase(e, c)
            attend_pe(e, c, "diff", HEADS1 // 2)
            phase(e, c)
            norm_pe(e, c, o_tile, HEADS1, ones, each=True)
            phase(e, c)
            mul_tiles(e, c, 2, DT, o_tile)
            phase(e, c)
            ln(x_tile)
            feed_forward()
            with c.loop(LAYERS2, LAYER) as l:
                e.wait_ge(layer_in, c.of("layer", 16, 16))
                settle(e)
                c.add("layer")
                mul_tiles(e, c, W_IN2_GROUPS, DT, x_tile)
                phase(e, c)
                for first in (DIL_Q, DIL_K):
                    rope_pe(e, c, 3, consts[:, C_ROT:C_ROT + P], lambda i, b: i * 2 + (first + b))
                phase(e, c)
                attend_pe(e, c, "dil", 2)
                phase(e, c)
                norm_pe(e, c, lambda j: big[:, CQ + j, :], 2, ones)
                norm_pe(e, c, lambda j: big[:, CKV + j, :], 1, ones)
                phase(e, c)
                mul_tiles(e, c, 1, 2, lambda k: big[:, CQ + k, :], rows=ROPE1)
                mul_tiles(e, c, 1, 1, lambda k: big[:, CKV + k, :])
                phase(e, c)
                rope_pe(e, c, 2, consts[:, C_ROTM:C_ROTM + P], lambda i, b: i * 2 + (MLA_Q + b))
                rope_pe(e, c, 1, consts[:, C_ROTM:C_ROTM + P], lambda i, b: MISC if b == 0 else MLA_Q + 4)
                phase(e, c)
                attend_pe(e, c, "mla", 2)
                attend_pe(e, c, "fox", 2)
                attend_pe(e, c, "sb", 2)
                phase(e, c)
                norm_pe(e, c, o_tile, DT, half1, each=True)
                phase(e, c)
                mul_tiles(e, c, 2, DT, o_tile)
                phase(e, c)
                ln(x_tile)
                route_pe(e)
                phase(e, c)
                spread_pe(e, c)
                phase(e, c)
                with c.loop(EXPERTS, {"group": 4}) as k:
                    for half in range(2):
                        for b in range(RING):
                            e.wait_ge(w_full[b], c.of("group", 16, 16))
                            e.wait_ge(bank_free[b], c.of("group", 1, 1))
                            for kt in range(DT):
                                m = e.matmul(ps[:, b, :], ring[:, b, kt * P:(kt + 1) * P], x[:, kt, :],
                                             start=kt == 0, stop=kt == DT - 1)
                            m.then_inc(tile_done[b], 1)
                        c.add("group")
                    for b in (1, 3):
                        e.wait_ge(bank_free[b], c.of("group", 1, 1))
                    for half in range(2):
                        for b in range(RING):
                            e.wait_ge(w_full[b], c.of("group", 16, 16))
                            e.wait_ge(bank_free[b], c.of("group", 1, 1))
                            for kt in range(ET):
                                m = e.matmul(ps[:, b, :], ring[:, b, kt * P:(kt + 1) * P], big[:, HID + kt, :],
                                             start=kt == 0, stop=kt == ET - 1)
                            m.then_inc(tile_done[b], 1)
                        c.add("group")
                phase(e, c)
                ln(o_tile)

        @block.scalar
        def _(e):
            c = Counts(e)
            e.sem_inc(exp_done, SETS)

            def ln(data, params, gain, shift):
                f = affine(params, gain, shift)
                norm_act(e, c, data, DT, centred=True, final=lambda e, j: f(e, j, data))
                phase(e, c)

            def col(name, j=0):
                return p1[:, COL1[name] + j:COL1[name] + j + 1]

            def take(turns, dst, scale=1.0, banks=(0, 2), func=ACT.Copy):
                with c.loop(turns, {"group": 1}) as i:
                    for b in banks:
                        e.wait_ge(tile_done[b], c.of("group", 1, 2))
                        e.activation(dst(i, b), ps[:, b, :], func, scale=scale).then_inc(bank_free[b], 1)
                    c.add("group")

            def take_one(b, dst, scale=1.0):
                e.wait_ge(tile_done[b], c.of("group", 1, 2))
                e.activation(dst, ps[0:dst.shape[0], b, :], ACT.Copy, scale=scale).then_inc(bank_free[b], 1)

            def feed_forward(layer):
                take(FT // 2, lambda i, b: big[:, i * 2 + b // 2, :], func=ACT.Silu)
                phase(e, c)
                c.add("group", 2)
                phase(e, c)
                ln(x_tile, p1, COL1[f"fg{layer}"], COL1[f"fb{layer}"])

            e.wait_ge(const_in, 6 * 16)
            e.activation(small[:, 8:12], p1[:, COL1["lam"]:COL1["lam"] + AT], ACT.Abs)
            e.drain()
            e.activation(small[:, 12:16], small[:, 8:12], ACT.Exp, scale=-1.0)
            e.drain()
            e.activation(small[:, 16:20], small[:, 12:16], ACT.Ln, bias=1.0)
            for j in range(AT):
                e.wait_ge(tile_done[0], c.of("group", 1, 2))
                e.activation(big[:, j, :], ps[:, 0, :], ACT.Sigmoid, bias=col("b_in", 4 * j)).then_inc(bank_free[0], 1)
                e.wait_ge(tile_done[2], c.of("group", 1, 2))
                e.activation(big[:, 4 + j, :], ps[:, 2, :], ACT.Gelu_apprx_tanh, bias=col("b_in", 4 * j + 2))\
                    .then_inc(bank_free[2], 1)
                c.add("group")
            phase(e, c)
            phase(e, c)
            e.activation(small[:, 20:22], small[:, 2:4], ACT.Exp)
            for j in range(AT):
                e.wait_ge(sg_ready, j + 1)
                e.activation(big[:, 16 + j, :], ps[:, j, :], ACT.Sigmoid, bias=col("b_a", j))
                e.activation(big[:, 20 + j, :], ps[:, 4 + j, :], ACT.Sigmoid, bias=col("b_x", j))
            e.drain()
            for j in range(AT):
                e.activation(big[:, 16 + j, :], big[:, 16 + j, :], ACT.Tanh, scale=small[:, 24 + j:25 + j])
            e.drain()
            e.activation(big[:, 24:28, :], big[:, 16:20, :], ACT.Sqrt)
            phase(e, c)
            norm_act(e, c, lambda j: big[:, 8 + j, :], AT, centred=True,
                     final=lambda e, j: e.activation(big[:, 8 + j, :], big[:, 8 + j, :], ACT.Silu, bias=col("cn_b", j),
                                                     scale=col("cn_g", j)))
            phase(e, c)
            c.add("group", 2)
            phase(e, c)
            ln(x_tile, p1, COL1["mg0"], COL1["mb0"])
            feed_forward(0)
            take(2, lambda i, b: big[:, i * RING + b, :], 0.125)
            take(4, lambda i, b: big[:, i * RING + (8 + b), :])
            phase(e, c)
            c.add("rope", HEADS1)
            phase(e, c)
            attend_act(e, c, "diff", HEADS1 // 2)
            phase(e, c)
            norm_act(e, c, o_tile, HEADS1, each=True)
            phase(e, c)
            c.add("group", 2)
            phase(e, c)
            ln(x_tile, p1, COL1["mg1"], COL1["mb1"])
            feed_forward(1)
            with c.loop(LAYERS2, LAYER) as l:
                e.wait_ge(layer_in, c.of("layer", 16, 16))
                settle(e)
                c.add("layer")
                take(2, lambda i, b: big[:, i * RING + b, :], 0.125)
                take_one(0, big[:, FOX_Q, :], 0.125)
                take_one(2, big[:, CQ, :])
                c.add("group")
                take(5, lambda i, b: big[:, i * RING + (DIL_K + b), :])
                take_one(0, big[:, CKV, :])
                take_one(2, o[:, 0, :])
                c.add("group")
                phase(e, c)
                phase(e, c)
                attend_act(e, c, "dil", 2)
                phase(e, c)
                norm_act(e, c, lambda j: big[:, CQ + j, :], 2)
                norm_act(e, c, lambda j: big[:, CKV + j, :], 1)
                f, g = probs[0:4, 0, 0:T], probs[0:4, 1, 0:T]
                e.activation(f, big[0:4, MISC, :], ACT.Identity, bias=p2[0:4, COL2["b_f"]:COL2["b_f"] + 1])
                e.drain()
                e.activation(g, f, ACT.Abs)
                e.drain()
                e.activation(g, g, ACT.Exp, scale=-1.0)
                e.drain()
                e.activation(g, g, ACT.Ln, bias=1.0).then_inc(kept_gate, 1)
                phase(e, c)
                for b in range(RING):
                    take_one(b, big[0:ROPE1, MLA_Q + b, :], float(ROPE1) ** -0.5)
                c.add("group")
                for b in (0, 2):
                    take_one(b, big[:, MLA_KV + b, :])
                c.add("group")
                phase(e, c)
                phase(e, c)
                attend_act(e, c, "mla", 2)
                attend_act(e, c, "fox", 2)
                attend_act(e, c, "sb", 2)
                phase(e, c)
                norm_act(e, c, o_tile, DT, each=True)
                phase(e, c)
                c.add("group", 2)
                phase(e, c)
                ln(x_tile, p2, COL2["ln1_g"], COL2["ln1_b"])
                phase(e, c)
                route_act(e, c)
                spread_act(e, c)
                phase(e, c)
                with c.loop(EXPERTS, {"group": 4}) as k:
                    for half in range(2):
                        for b in (0, 2):
                            e.wait_ge(tile_done[b], c.of("group", 1, 2))
                            e.activation(big[:, HID + 2 * half + b // 2, :], ps[:, b, :], ACT.Silu)\
                                .then_inc(bank_free[b], 1)
                        c.add("group")
                    c.add("group", 2)
                phase(e, c)
                ln(o_tile, p2, COL2["ln2_g"], COL2["ln2_b"])

        @block.vector
        def _(e):
            c = Counts(e)

            def ln(data):
                norm_dve(e, c, data, DT, D, LN_EPS, centred=True)
                phase(e, c)

            def col(name, j=0):
                return p1[:, COL1[name] + j:COL1[name] + j + 1]

            def add_to_x():
                with c.loop(2, {"group": 1}) as i:
                    for b in range(RING):
                        e.wait_ge(tile_done[b], c.of("group", 1, 2))
                        e.scalar_tensor_tensor(x[:, i * RING + b, :], x[:, i * RING + b, :], ALPHA, ps[:, b, :],
                                               ALU.mult, ALU.add).then_inc(bank_free[b], 1)
                    c.add("group")
                phase(e, c)

            def feed_forward():
                with c.loop(FT // 2, {"group": 1}) as i:
                    for b in (1, 3):
                        e.wait_ge(tile_done[b], c.of("group", 1, 2))
                        e.wait_ge(bank_free[b - 1], c.of("group", 1, 2))
                        h = big[:, i * 2 + b // 2, :]
                        e.tensor_tensor(h, h, ps[:, b, :], ALU.mult).then_inc(bank_free[b], 1)
                    c.add("group")
                phase(e, c)
                add_to_x()
                ln(x_tile)

            def take(turns, dst, scale=1.0):
                with c.loop(turns, {"group": 1}) as i:
                    for b in (1, 3):
                        e.wait_ge(tile_done[b], c.of("group", 1, 2))
                        e.tensor_scalar(dst(i, b), ps[:, b, :], scale, None, ALU.mult).then_inc(bank_free[b], 1)
                    c.add("group")

            def take_one(b, dst, scale=1.0):
                e.wait_ge(tile_done[b], c.of("group", 1, 2))
                e.tensor_scalar(dst, ps[:, b, :], scale, None, ALU.mult).then_inc(bank_free[b], 1)

            def taps(src, width, weights, bias, dst):
                for j in range(AT):
                    e.tensor_scalar(dst(j), src(j, 0), col(weights, j), col(bias, j), ALU.mult, ALU.add)
                for k in range(1, width):
                    e.drain()
                    for j in range(AT):
                        e.scalar_tensor_tensor(dst(j), src(j, k), col(weights, AT * k + j), dst(j), ALU.mult, ALU.add)

            e.wait_ge(const_in, 6 * 16)
            e.memset(u_buf[:, :, 0:CONV - 1], 0.0)
            e.memset(rec[:, :, 0:LCONV - 1], 0.0)
            for j in range(AT):
                e.wait_ge(tile_done[1], c.of("group", 1, 2))
                e.wait_ge(bank_free[0], c.of("group", 1, 2))
                e.scalar_tensor_tensor(u_buf[:, j, CONV - 1:CONV - 1 + T], ps[:, 1, :], col("b_in", 4 * j + 1),
                                       big[:, j, :], ALU.add, ALU.mult).then_inc(bank_free[1], 1)
                e.wait_ge(tile_done[3], c.of("group", 1, 2))
                e.tensor_scalar(rec[:, j, LCONV - 1:LCONV - 1 + T], ps[:, 3, :], col("b_in", 4 * j + 3), None, ALU.add)\
                    .then_inc(bank_free[3], 1)
                c.add("group")
            phase(e, c)
            taps(lambda j, k: rec[:, j, k:k + T], LCONV, "lconv_w", "lconv_b", lambda j: big[:, 12 + j, :])
            e.tensor_scalar(small[:, 24:28], p1[:, COL1["lam"]:COL1["lam"] + AT], -1.0, 0.0, ALU.mult, ALU.max)
            lamv = p1[:, COL1["lamv"]:COL1["lamv"] + 256].rearrange("p (a b d) -> p a b d", a=2, b=2)
            dots = scan[:, 0:P].rearrange("p (a d) -> p a d", a=2)
            e.tensor_tensor(dots, lamv[:, :, 0, :], lamv[:, :, 1, :], ALU.mult)
            e.tensor_scalar(small[:, 5:6], col("subln"), 1.0 - LAMBDA_INIT, None, ALU.mult)
            e.drain()
            e.tensor_tensor(small[:, 24:28], small[:, 24:28], small[:, 16:20], ALU.add)
            e.tensor_reduce(small[:, 2:4], dots, AX.X, ALU.add)
            e.drain()
            e.tensor_scalar(small[:, 24:28], small[:, 24:28], 4.0, None, ALU.mult)
            phase(e, c)
            taps(lambda j, k: u_buf[:, j, k:k + T], CONV, "conv_w", "conv_b", lambda j: big[:, 8 + j, :])
            phase(e, c)
            e.tensor_tensor(small[:, 4:5], small[:, 21:22], small[:, 20:21], ALU.subtract)
            e.drain()
            e.tensor_scalar(small[:, 4:5], small[:, 4:5], LAMBDA_INIT, None, ALU.subtract)
            norm_dve(e, c, lambda j: big[:, 8 + j, :], AT, AT * P, LN_EPS, centred=True)
            h, gi, root, den = big[:, 16:20, :], big[:, 20:24, :], big[:, 24:28, :], big[:, 28:32, :]
            e.tensor_scalar(den, h, 1.0, None, ALU.add)
            e.tensor_tensor(gi, gi, big[:, 12:16, :], ALU.mult)
            e.drain()
            e.reciprocal(den, den)
            e.tensor_scalar(h, h, -1.0, 1.0, ALU.mult, ALU.add)
            e.tensor_tensor(gi, gi, root, ALU.mult)
            e.drain()
            e.tensor_tensor(h, h, den, ALU.mult)
            for j in range(AT):
                e.scalar_tensor_tensor(gi[:, j, :], gi[:, j, :], 2.0, den[:, j, :], ALU.mult, ALU.mult)
            e.drain()
            for j in range(AT):
                e.tensor_tensor_scan(root[:, j, :], h[:, j, :], gi[:, j, :], 0.0, ALU.mult, ALU.add)
            e.drain()
            e.tensor_tensor(big[:, 12:16, :], root, big[:, 4:8, :], ALU.mult)
            phase(e, c)
            add_to_x()
            ln(x_tile)
            feed_forward()
            take(2, lambda i, b: big[:, i * RING + b, :], 0.125)
            take(4, lambda i, b: big[:, i * RING + (8 + b), :])
            phase(e, c)
            rope_dve(e, c, HEADS1, tabs[:, 0, :], tabs[:, 1, :], lambda i, b: i * 2 + b)
            phase(e, c)
            attend_dve(e, c, "diff", HEADS1 // 2, 0)
            phase(e, c)
            norm_dve(e, c, o_tile, HEADS1, P, LN_EPS, each=True, scaled=lambda j: small[:, 5:6])
            phase(e, c)
            add_to_x()
            ln(x_tile)
            feed_forward()
            with c.loop(LAYERS2, LAYER) as l:
                e.wait_ge(layer_in, c.of("layer", 16, 16))
                settle(e)
                c.add("layer")
                take(2, lambda i, b: big[:, i * RING + b, :], 0.125)
                take_one(1, big[:, FOX_Q + 1, :], 0.125)
                take_one(3, big[:, CQ + 1, :])
                c.add("group")
                take(5, lambda i, b: big[:, i * RING + (DIL_K + b), :])
                take_one(1, big[:, MISC, :])
                take_one(3, o[:, 1, :])
                c.add("group")
                phase(e, c)
                for first in (DIL_Q, DIL_K):
                    rope_dve(e, c, 3, tabs[:, 0, :], tabs[:, 1, :], lambda i, b: i * 2 + (first + b))
                phase(e, c)
                attend_dve(e, c, "dil", 2, 6)
                phase(e, c)
                norm_dve(e, c, lambda j: big[:, CQ + j, :], 2, 2 * P, RMS_EPS,
                         scaled=lambda j: p2[:, COL2["g_cq"] + j:COL2["g_cq"] + j + 1])
                e.drain()
                norm_dve(e, c, lambda j: big[:, CKV + j, :], 1, P, RMS_EPS,
                         scaled=lambda j: p2[:, COL2["g_ckv"]:COL2["g_ckv"] + 1])
                e.wait_ge(kept_gate, c.of("fox", 1, 1))
                c.add("fox")
                f, g = probs[0:4, 0, :], probs[0:4, 1, :]
                e.scalar_tensor_tensor(f[:, 0:T], f[:, 0:T], 0.0, g[:, 0:T], ALU.min, ALU.subtract)
                e.drain()
                e.tensor_tensor_scan(f[:, T:2 * T], f[:, 0:T], f[:, 0:T], 0.0, ALU.add, ALU.bypass)
                e.memset(big[64:65, FOX_C, :], 1.0)
                e.drain()
                e.tensor_scalar(g[:, T:2 * T], f[:, T:2 * T], -1.0, None, ALU.mult)
                phase(e, c)
                c.add("group")
                for b in (1, 3):
                    take_one(b, big[:, MLA_KV + b, :])
                c.add("group")
                phase(e, c)
                cosm, sinm = tabs[:, 2, :], tabs[:, 3, :]
                rope_dve(e, c, 2, cosm, sinm, lambda i, b: i * 2 + (MLA_Q + b))
                rope_dve(e, c, 1, cosm, sinm, lambda i, b: MISC if b == 0 else MLA_Q + 4)
                phase(e, c)
                attend_dve(e, c, "mla", 2, 4)
                attend_dve(e, c, "fox", 2, 2)
                attend_dve(e, c, "sb", 2, 0)
                phase(e, c)
                norm_dve(e, c, o_tile, DT, 64, RMS_EPS, each=True,
                         scaled=lambda j: p2[:, COL2["g_head"] + j:COL2["g_head"] + j + 1])
                phase(e, c)
                add_to_x()
                ln(x_tile)
                phase(e, c)
                route_dve(e, c)
                phase(e, c)
                with c.loop(EXPERTS, {"group": 4}) as k:
                    for half in range(2):
                        for b in (1, 3):
                            e.wait_ge(tile_done[b], c.of("group", 1, 2))
                            e.wait_ge(bank_free[b - 1], c.of("group", 1, 2))
                            h = big[:, HID + 2 * half + b // 2, :]
                            e.tensor_tensor(h, h, big[:, k + GATE, :], ALU.mult)
                            e.drain()
                            e.tensor_tensor(h, h, ps[:, b, :], ALU.mult).then_inc(bank_free[b], 1)
                        c.add("group")
                    for half in range(2):
                        for b in range(RING):
                            e.wait_ge(tile_done[b], c.of("group", 1, 2))
                            y = o[:, RING * half + b, :]
                            e.tensor_tensor(y, y, ps[:, b, :], ALU.add).then_inc(bank_free[b], 1)
                        c.add("group")
                phase(e, c)
                ln(o_tile)


def rotation(rows):
    r = np.zeros((P, P), np.float32)
    for start, width in rows:
        half = width // 2
        for d in range(half):
            r[start + half + d, start + d] = -1.0
            r[start + d, start + half + d] = 1.0
    return r


def constants():
    q, k = np.arange(P)[:, None], np.arange(P)[None, :]
    q4, k4 = q + T - P, np.arange(T)[None, :]
    masks = np.zeros((P, M_COLS), np.float32)
    masks[:, M_BAND:M_BAND + P] = np.where(k >= q, 0, NEG)
    masks[:, M_TRI:M_TRI + P] = np.where(k <= q, 0, NEG)
    masks[:, M_MOD4:M_MOD4 + T] = np.where((k4 <= q4) & ((q4 - k4) % 4 == 0), 0, NEG)
    masks[:, M_MOD16:M_MOD16 + T] = np.where((k4 <= q4) & ((q4 - k4) % 16 == 0), 0, NEG)
    masks[:, M_CHUNK:M_CHUNK + P] = np.where(k // 64 <= q // 64, 0, NEG)
    masks[:, M_STRICT:M_STRICT + P] = np.where(k < q, 0, NEG)
    masks[:, M_KEEP:M_KEEP + P] = np.where(k < q, 1, 0)
    consts = np.zeros((P, C_COLS), np.float32)
    consts[:, C_ID:C_ID + P] = np.eye(P)
    consts[:, C_ONE:C_ONE + P] = 1.0
    consts[:, C_HALF:C_HALF + P] = q // 64 == k // 64
    consts[:, C_ROT:C_ROT + P] = rotation([(0, 64), (64, 64)])
    consts[:, C_ROTM:C_ROTM + P] = rotation([(ROPE0, ROPE1 - ROPE0)])
    consts[:, C_IOTA:C_IOTA + EXPERTS] = np.arange(EXPERTS)
    tabs = np.zeros((P, 4, T), np.float32)
    tabs[:, 2, :] = 1.0

    def angles(half):
        inv = np.float32(10000.0) ** (-np.arange(half, dtype=np.float32) / np.float32(half))
        ang = np.arange(T, dtype=np.float32)[None, :] * inv.astype(np.float32)[:, None]
        return np.cos(ang), np.sin(ang)

    cos, sin = angles(32)
    tabs[:, 0, :], tabs[:, 1, :] = np.tile(cos, (4, 1)), np.tile(sin, (4, 1))
    cos, sin = angles(16)
    tabs[ROPE0:ROPE1, 2, :], tabs[ROPE0:ROPE1, 3, :] = np.tile(cos, (2, 1)), np.tile(sin, (2, 1))
    return masks, consts, tabs


def by_tile(w, cols=P):
    *lead, k, n = w.shape
    m = len(lead)
    w = w.reshape(*lead, k // P, P, n // cols, cols)
    w = np.transpose(w, (*range(m), m + 2, m + 1, m, m + 3))
    return np.ascontiguousarray(w).reshape(*lead, n // cols, P, (k // P) * cols)


def by_column(v):
    return v.reshape(-1, P).T


def pack(parts):
    return np.ascontiguousarray(np.concatenate(parts, axis=1))


def lay_out(i):
    g = {k: np.asarray(v) for k, v in i.items()}
    masks, consts, tabs = constants()
    order = [b * AT + j for j in range(AT) for b in (1, 0, 2, 3)]
    w_in = by_tile(g["even_w_in"][0])[order]
    b_in = g["even_b_in"][0].reshape(16, P)[order].reshape(-1)
    gates = np.zeros((P, 2 * AT, P), np.float32)
    for n, name in enumerate(("even_w_a", "even_w_x")):
        for j in range(AT):
            for s in range(2):
                gates[64 * s:64 * s + 64, AT * n + j, 64 * s:64 * s + 64] = g[name][0, 2 * j + s]
    lamv = np.concatenate([g[f"odd_lambda_{v}"][0] for v in ("q1", "k1", "q2", "k2")])
    p1 = pack([by_column(b_in), by_column(g["even_conv_w"][0]), by_column(g["even_conv_b"][0]),
               by_column(g["even_cnorm_g"][0]), by_column(g["even_cnorm_b"][0]), by_column(g["even_lru_conv_w"][0]),
               by_column(g["even_lru_conv_b"][0]), by_column(g["even_b_a"][0]), by_column(g["even_b_x"][0]),
               by_column(g["even_lru_lambda"][0]), by_column(g["odd_subln_g"][0]),
               np.broadcast_to(lamv[None, :], (P, 256))]
              + [by_column(g[f"{w}_ln_{v}"][l]) for l in range(DEPTH) for w in ("mix", "ffn") for v in ("g", "b")])
    w2 = g["w_in_2"]
    at = {"sb": 0, "fox": 768, "f": 1536, "cq": 1540, "ckv": 1796, "kr": 1924, "dil": 1956}
    misc = np.zeros((LAYERS2, D, 3 * P), np.float32)
    misc[:, :, 0:4] = w2[:, :, at["f"]:at["f"] + 4]
    misc[:, :, ROPE0:ROPE1] = w2[:, :, at["kr"]:at["kr"] + 32]

    def cut(name, first, n):
        return w2[:, :, at[name] + first:at[name] + first + n]

    w_in2 = np.concatenate([cut("dil", 0, 768), cut("sb", 0, 256), cut("fox", 0, 256), cut("cq", 0, 256),
                            cut("dil", 768, 768), cut("sb", 256, 256), cut("fox", 256, 256), cut("dil", 1536, 768),
                            cut("sb", 512, 256), cut("fox", 512, 256), cut("ckv", 0, 128), misc], axis=2)
    b_f = np.zeros((LAYERS2, P, 1), np.float32)
    b_f[:, 0:4, 0] = g["b_forget_2"]
    router = np.concatenate([g["w_group_2"], g["w_expert_2"]], axis=2)
    router_b = np.concatenate([g["b_group_2"], g["b_expert_2"]], axis=1)
    p2 = np.stack([pack([by_column(g["g_cq_2"][l]), by_column(g["g_ckv_2"][l]), by_column(g["g_head_2"][l]),
                         by_column(g["ln1_g_2"][l]), by_column(g["ln1_b_2"][l]), by_column(g["ln2_g_2"][l]),
                         by_column(g["ln2_b_2"][l]), b_f[l],
                         router[l].reshape(DT, P, 20).transpose(1, 0, 2).reshape(P, DT * 20),
                         np.broadcast_to(router_b[l][None, :], (P, 20))]) for l in range(LAYERS2)])
    return {
        "x": np.ascontiguousarray(g["x"][0].T.reshape(DT, P, T).transpose(1, 0, 2)),
        "p1": p1, "p2": p2, "consts": consts, "masks": masks, "tabs": tabs, "gates": gates,
        "w_in": np.ascontiguousarray(w_in), "w_out": by_tile(g["even_w_out"][0]),
        "w_gate": by_tile(g["ffn_w_gate"]), "w_up": by_tile(g["ffn_w_up"]), "w_down": by_tile(g["ffn_w_down"]),
        "w_qkv": by_tile(g["odd_w_qkv"][0]), "w_out1": by_tile(g["odd_w_out"][0]),
        "w_in2": by_tile(w_in2), "w_uq": by_tile(g["w_uq_2"], ROPE1), "w_ukv": by_tile(g["w_ukv_2"]),
        "w_out2": by_tile(g["w_out_2"]), "w1": by_tile(g["w1_2"]), "w3": by_tile(g["w3_2"]), "w2": by_tile(g["w2_2"]),
    }


def kernel(**inputs):
    import concourse.bacc as bacc
    from concourse.bass_utils import run_bass_kernel_spmd

    nc = bacc.Bacc("TRN2", target_bir_lowering=False, num_devices=1)
    arrays = lay_out(inputs)
    a = {name: nc.dram_tensor(name, v.shape, F32, kind="ExternalInput").ap() for name, v in arrays.items()}
    out = nc.dram_tensor("out", (P, DT, T), F32, kind="ExternalOutput").ap()
    build(nc, a, out)
    r = run_bass_kernel_spmd(nc, [arrays], core_ids=[0])
    y = np.asarray(r.results[0]["out"])
    return np.ascontiguousarray(y.transpose(1, 0, 2).reshape(D, T).T).reshape(1, T, D)
```

```python
from contextlib import ExitStack, contextmanager

import numpy as np

import concourse.bass as bass
from concourse import mybir

F32 = mybir.dt.float32
F32R = mybir.dt.float32r
U32 = mybir.dt.uint32
ALU = mybir.AluOpType
ACT = mybir.ActivationFunctionType
AX = mybir.AxisListType

P = 128
T = 512
D = 1024
DT = D // P
QB = T // P
DEPTH = 2
FF = 2816
FT = FF // P
AT = 4
CONV = 31
LCONV = 4
HEADS1 = 8
ALPHA = (2 * DEPTH) ** 0.25
LAMBDA_INIT = 0.8 - 0.6 * float(np.exp(-0.3))
LN_EPS = 1e-5
RMS_EPS = 1e-6
NEG = -1e30
EXPERTS = 16
GROUPS = 4
ET = 4
RING = 4
SLOT = FT * P // 2
BIG = 34
LAYERS2 = 2

DIL_Q, SB_Q, FOX_Q, CQ = 0, 6, 8, 10
DIL_K, SB_K, FOX_K = 12, 18, 20
DIL_V, SB_V, FOX_V = 22, 28, 30
CKV, MISC = 32, 33
W_IN2_GROUPS = 9
MLA_Q, MLA_KV, FOX_C = 0, 12, 22
ROPE0, ROPE1 = 64, 96

M_BAND, M_TRI, M_MOD4, M_MOD16, M_CHUNK, M_STRICT, M_KEEP = 0, 128, 256, 768, 1280, 1408, 1536
M_COLS = 1664
C_ID, C_ONE, C_HALF, C_ROT, C_ROTM = 0, 128, 256, 384, 512
C_IOTA = 640
C_COLS = 656

PARAM1 = [("b_in", 16), ("conv_w", CONV * AT), ("conv_b", AT), ("cn_g", AT), ("cn_b", AT), ("lconv_w", LCONV * AT),
          ("lconv_b", AT), ("b_a", AT), ("b_x", AT), ("lam", AT), ("subln", 1), ("lamv", 256),
          ("mg0", DT), ("mb0", DT), ("fg0", DT), ("fb0", DT), ("mg1", DT), ("mb1", DT), ("fg1", DT), ("fb1", DT)]
PARAM2 = [("g_cq", 2), ("g_ckv", 1), ("g_head", DT), ("ln1_g", DT), ("ln1_b", DT), ("ln2_g", DT), ("ln2_b", DT),
          ("b_f", 1), ("router", DT * 20), ("router_b", 20)]


def columns(table):
    at, out = 0, {}
    for name, n in table:
        out[name] = at
        at += n
    return out, at


COL1, NP1 = columns(PARAM1)
COL2, NP2 = columns(PARAM2)


class Counts:

    def __init__(self, eng):
        self.eng, self.n, self.turns = eng, {}, []

    def of(self, event, scale=1, more=0):
        total = self.n.get(event, 0) * scale + more
        for reg, per in self.turns:
            if per.get(event):
                total = reg * (per[event] * scale) + total
        return total

    def add(self, event, k=1):
        self.n[event] = self.n.get(event, 0) + k

    @contextmanager
    def loop(self, turns, per):
        before = dict(self.n)
        with self.eng.Fori(0, turns) as i:
            self.turns.append((i, per))
            yield i
            self.turns.pop()
        for event in self.n:
            assert self.n[event] - before.get(event, 0) in (0, per.get(event, 0)), (event, self.n, before, per)
        self.n = {e: before.get(e, 0) + turns * per.get(e, 0) for e in {**self.n, **per}}


def steps_of(kind):
    plan = []
    for qb in range(QB):
        if kind == "dil":
            lo = max(qb - 1, 0)
            segs = [(0, 0, 64, lo, qb + 1 - lo, M_TRI + P - P * (qb + 1 - lo)),
                    (1, 0, 64, 0, qb + 1, M_MOD4 + T - P * (qb + 1)),
                    (2, 0, 64, 0, qb + 1, M_MOD16 + T - P * (qb + 1))]
        elif kind == "diff":
            segs = [(None, 64 * m, 64 * m + 64, 0, qb + 1, M_CHUNK) for m in range(2)]
        else:
            rows = {"sb": 64, "fox": 66, "mla": 96}[kind]
            segs = [(None, 0, rows, 0, qb + 1, None if kind == "sb" else M_TRI)]
        plan.append(segs)
    return plan


def blocks_of(kind, segs):
    if kind == "diff":
        return [(0, b) for b in range(segs[0][4])]
    return [(s, b) for s, seg in enumerate(segs) for b in range(seg[4])]


def t_turns(kind):
    values = 3 if kind == "dil" else 1
    return 2 * (values + sum(-(-len(blocks_of(kind, s)) // 4) for s in steps_of(kind)))


PAIR = {"steps": 2 * QB}
STAGED = {"dil": 9, "diff": 3, "sb": 3, "fox": 7, "mla": 4}


def build(nc, a, out):
    es = ExitStack()
    with es:
        def sb(name, *shape, dt=F32):
            return es.enter_context(nc.sbuf_tensor("sb_" + name, list(shape), dt))

        def sem(name):
            return es.enter_context(nc.semaphore(name))

        x = sb("x", P, DT, T)
        ring = sb("ring", P, RING, SLOT)
        w_hi = sb("w_hi", P, 2, SLOT, dt=F32R)
        w_lo = sb("w_lo", P, 2, SLOT, dt=F32R)
        tabs = sb("tabs", P, 4, T)
        masks = sb("masks", P, M_COLS)
        consts = sb("consts", P, C_COLS)
        p1 = sb("p1", P, NP1)
        p2 = sb("p2", P, NP2)
        stat = sb("stat", P, 2, 16)
        small = sb("small", P, 40)
        route = sb("route", P, QB, 96)
        picks = sb("picks", P, QB, 8, dt=U32)
        arena = es.enter_context(nc.sbuf_tensor("arena", [P, 2560 + 1280 + 512 + 1024 + (BIG + 10 + DT) * T], F32))
        base = nc.sbuf_base - 4 * arena.shape[1]

        def at(name, offset, *shape, dt=F32):
            return nc.alloc_sbuf_tensor_at("at_" + name, list(shape), dt, offset=base + 4 * offset)

        probs = at("probs", 0, P, 2, 1280)
        probs_t = at("probs_t", 2560, P, 10, P)
        scan = at("scan", 3840, P, T)
        vtok = at("vtok", 4352, P, 1024)
        big_at = 5376
        big = at("big", big_at, P, BIG, T)
        shared_at = big_at + BIG * T
        shared = at("shared", shared_at, P, 10, T)
        o_at = shared_at + 10 * T
        o = at("o", o_at, P, DT, T)
        h_hi = at("h_hi", 0, P, FT, T, dt=F32R)
        h_lo = at("h_lo", FT * T, P, FT, T, dt=F32R)
        h_raw = shared[:, 0:2, :]
        high = (at("high_hi", shared_at + 2 * T, P, DT, T, dt=F32R), at("high_lo", o_at, P, DT, T, dt=F32R))
        low = (at("low_hi", big_at + 16 * T, P, DT, T, dt=F32R), at("low_lo", big_at + 24 * T, P, DT, T, dt=F32R))
        eh_hi = at("eh_hi", shared_at + 2 * T, P, ET, T, dt=F32R)
        eh_lo = at("eh_lo", shared_at + 6 * T, P, ET, T, dt=F32R)
        sq = shared
        st_q, st_k, st_v = shared[:, 0:3, :], shared[:, 3:6, :], shared[:, 6:9, :]
        u_buf = o[:, :, :].rearrange("p a t -> p (a t)")[:, 0:AT * 544].rearrange("p (j t) -> p j t", t=544)
        rec = shared[:, :, :].rearrange("p a t -> p (a t)")[:, 0:AT * 520].rearrange("p (j t) -> p j t", t=520)
        gates_w = probs[:, :, :].rearrange("p a t -> p (a t)")[:, 0:1024].rearrange("p (j t) -> p j t", t=P)
        row = shared[:, 9, :]

        ident, ones = consts[:, C_ID:C_ID + P], consts[:, C_ONE:C_ONE + P]
        half1 = consts[:, C_HALF:C_HALF + P]
        ps = es.enter_context(nc.psum_tensor("ps", [P, 8, T], F32))

        w_full = [sem(f"w_full{b}") for b in range(RING)]
        tile_done = [sem(f"tile_done{b}") for b in range(RING)]
        bank_free = [sem(f"bank_free{b}") for b in range(RING)]
        hi_done = [sem(f"hi_done{b}") for b in range(RING)]
        slot_split = [sem(f"slot_split{b}") for b in range(RING)]
        act_hi = sem("act_hi")
        act_split = sem("act_split")
        hid_done = sem("hid_done")
        phase_done = sem("phase_done")
        const_in = sem("const_in")
        settled = sem("settled")
        layer_in = sem("layer_in")
        gates_in = sem("gates_in")
        sg_ready = sem("sg_ready")
        norm_sum = sem("norm_sum")
        norm_dev = sem("norm_dev")
        norm_sq = sem("norm_sq")
        norm_var = sem("norm_var")
        norm_inv = sem("norm_inv")
        norm_rstd = sem("norm_rstd")
        norm_out = sem("norm_out")
        rot_full = [sem(f"rot_full{b}") for b in range(2)]
        rot_free = [sem(f"rot_free{b}") for b in range(2)]
        staged = [sem(f"staged{b}") for b in range(2)]
        scored = sem("scored")
        kept = sem("kept")
        max_ready = sem("max_ready")
        exp_done = sem("exp_done")
        p_ready = sem("p_ready")
        o_full = sem("o_full")
        o_free = sem("o_free")
        t_full = sem("t_full")
        t_free = sem("t_free")
        fox_rows = sem("fox_rows")
        kept_gate = sem("kept_gate")
        route_in = sem("route_in")
        route_exp = sem("route_exp")
        spread_in = sem("spread_in")
        spread_full = [sem(f"spread_full{b}") for b in range(2)]
        spread_free = [sem(f"spread_free{b}") for b in range(2)]
        out_done = sem("out_done")

        ENGINES = 3

        def settle(e):
            e.sem_inc(settled, 1)

        def phase_wait(e, c):
            e.wait_ge(phase_done, c.of("phase", ENGINES))
            settle(e)

        def phase(e, c):
            settle(e)
            e.drain()
            e.sem_inc(phase_done, 1)
            c.add("phase")
            phase_wait(e, c)

        def load_tiles(e, c, groups, srcs, width):
            with c.loop(groups, {"group": 1}) as i:
                for b in range(RING):
                    e.wait_ge(slot_split[b], c.of("group", 1, 1))
                    src = srcs(i, b)
                    e.dma_start(ring[:, b, 0:width], src).then_inc(w_full[b], 16)
                c.add("group")

        def split_act(e, c, width, b, ahead):
            e.wait_ge(w_full[b], c.of("group", 16, 16 + 16 * ahead))
            e.activation(w_hi[:, b % 2, 0:width], ring[:, b, 0:width], ACT.Copy).then_inc(hi_done[b], 1)

        def split_dve(e, c, width, b, ahead):
            e.wait_ge(hi_done[b], c.of("group", 1, 1 + ahead))
            e.tensor_tensor(w_lo[:, b % 2, 0:width], ring[:, b, 0:width], w_hi[:, b % 2, 0:width].bitcast(F32),
                            ALU.subtract).then_inc(slot_split[b], 1)

        def take_tiles(e, c, groups, split, width, take, start=True, end=True, loop=True):
            def group(i, last):
                for b in range(RING):
                    e.wait_ge(tile_done[b], c.of("group", 1, 2))
                    m = take(i, b)
                    if m is not None:
                        m.then_inc(bank_free[b], 1)
                    if b < 2 or not last:
                        split(e, c, width, (b + 2) % RING, b // 2)
                c.add("group")

            if start:
                for b in range(2):
                    split(e, c, width, b, 0)
            turns = groups - 1 if end else groups
            if turns > 1 and loop:
                with c.loop(turns, {"group": 1}) as i:
                    group(i, False)
            else:
                for i in range(turns):
                    group(i, False)
            if end:
                group(groups - 1, True)

        def hidden_tiles(e, c, split, take):
            for b in range(2):
                split(e, c, DT * P, b, 0)

            def group(i, last):
                for b in range(RING):
                    e.wait_ge(tile_done[b], c.of("group", 1, 2))
                    m = take(i, b)
                    if m is not None:
                        m.then_inc(bank_free[b], 1)
                    if b < 2 or not last:
                        split(e, c, DT * P, (b + 2) % RING, b // 2)
                c.add("group")

            with c.loop(FT // 2 - 1, {"group": 1, "hidden": 2}) as i:
                group(i, False)
            group(FT // 2 - 1, True)

        def expert_tiles(e, c, split, take):
            def group(k, g, last):
                width = DT * P if g < 2 else ET * P
                ahead = DT * P if g in (0, 3) else ET * P
                for b in range(RING):
                    e.wait_ge(tile_done[b], c.of("group", 1, 2))
                    m = take(k, g, b)
                    if m is not None:
                        m.then_inc(bank_free[b], 1)
                    if b < 2:
                        split(e, c, width, b + 2, 0)
                    elif not last:
                        split(e, c, ahead, b - 2, 1)
                c.add("group")

            for b in range(2):
                split(e, c, DT * P, b, 0)
            with c.loop(EXPERTS - 1, {"group": 4, "hidden": ET}) as k:
                for g in range(4):
                    group(k, g, False)
            for g in range(4):
                group(EXPERTS - 1, g, g == 3)

        def mul3(e, out_, k, cols, b, rhs_hi, rhs_lo, start, stop):
            hi, lo = w_hi[:, b % 2, k * cols:(k + 1) * cols], w_lo[:, b % 2, k * cols:(k + 1) * cols]
            e.matmul(out_, hi, rhs_hi, start=start, stop=False)
            e.matmul(out_, hi, rhs_lo, start=False, stop=False)
            return e.matmul(out_, lo, rhs_hi, start=False, stop=stop)

        def mul_tiles(e, c, groups, halves):
            with c.loop(groups, {"group": 1}) as i:
                for b in range(RING):
                    e.wait_ge(slot_split[b], c.of("group", 1, 2))
                    e.wait_ge(bank_free[b], c.of("group", 1, 1))
                    for k in range(DT):
                        m = mul3(e, ps[:, b, :], k, P, b, halves[0][:, k, :], halves[1][:, k, :], k == 0, k == DT - 1)
                    m.then_inc(tile_done[b], 1)
                c.add("group")

        def halve_act(e, c, halves, src):
            for j in range(DT):
                e.activation(halves[0][:, j, :], src(j), ACT.Copy).then_inc(act_hi, 1)

        def halve_dve(e, c, halves, src):
            for j in range(DT):
                e.wait_ge(act_hi, c.of("halves", 1, j + 1))
                e.tensor_tensor(halves[1][:, j, :], src(j), halves[0][:, j, :].bitcast(F32), ALU.subtract)\
                    .then_inc(act_split, 1)
            c.add("halves", DT)

        def halve_pe(e, c):
            e.wait_ge(act_split, c.of("halves", 1, DT))
            settle(e)
            c.add("halves", DT)

        def silu_act(e, c, b, j):
            e.wait_ge(hid_done, c.of("hidden", 1, 1))
            c.add("hidden")
            return e.activation(h_raw[:, j % 2, :], ps[:, b, :], ACT.Silu)

        def hidden_dve(e, c, b, j, hi, lo, gate=None):
            e.wait_ge(bank_free[b - 1], c.of("group", 1, 2))
            c.add("hidden")
            h = h_raw[:, j % 2, :]
            e.tensor_tensor(h, h, ps[:, b, :], ALU.mult).then_inc(bank_free[b], 1)
            e.drain()
            if gate is not None:
                e.tensor_tensor(h, h, gate, ALU.mult)
                e.drain()
            e.tensor_copy(hi, h)
            e.drain()
            e.tensor_tensor(lo, h, hi.bitcast(F32), ALU.subtract).then_inc(hid_done, 1)

        def norm_pe(e, c, data, n, avg, centred=False, each=False):
            if centred:
                for j in range(n):
                    m = e.matmul(ps[:, 4, :], avg, data(j), start=j == 0, stop=j == n - 1)
                m.then_inc(norm_sum, 1)
            for j in range(n):
                e.wait_ge(norm_sq, c.of("norm_sq", 1, j + 1))
                if each and j >= 2:
                    e.wait_ge(norm_inv, c.of("norm_inv", 1, j - 1))
                m = e.matmul(ps[:, 5 + (j % 2 if each else 0), :], avg, sq[:, j, :],
                             start=each or j == 0, stop=each or j == n - 1)
                if each or j == n - 1:
                    m.then_inc(norm_var, 1)
            c.add("norm_sq", n)
            c.add("norm_inv", n if each else 1)

        def norm_dve(e, c, data, n, width, eps, centred=False, each=False, scaled=None):
            if centred:
                e.wait_ge(norm_sum, c.of("norm_sum", 1, 1))
                c.add("norm_sum")
                for j in range(n):
                    e.scalar_tensor_tensor(data(j), ps[:, 4, :], -1.0 / width, data(j), ALU.mult,
                                           ALU.add).then_inc(norm_dev, 1)
            for g in range(n if each else 1):
                e.wait_ge(norm_var, c.of("norm_var", 1, 1))
                if g:
                    settle(e)
                    e.drain()
                e.tensor_scalar(row, ps[:, 5 + g % 2, :], 1.0 / width, eps, ALU.mult, ALU.add)
                e.drain()
                e.reciprocal(row, row).then_inc(norm_inv, 1)
                e.wait_ge(norm_rstd, c.of("norm_rstd", 1, 1))
                c.add("norm_var")
                c.add("norm_rstd")
                for j in [g] if each else range(n):
                    if scaled:
                        e.scalar_tensor_tensor(data(j), data(j), scaled(j), row, ALU.mult, ALU.mult)
                    else:
                        e.tensor_tensor(data(j), data(j), row, ALU.mult).then_inc(norm_out, 1)

        def norm_act(e, c, data, n, centred=False, each=False, final=None):
            for j in range(n):
                if centred:
                    e.wait_ge(norm_dev, c.of("norm_dev", 1, j + 1))
                e.activation(sq[:, j, :], data(j), ACT.Square).then_inc(norm_sq, 1)
            if centred:
                c.add("norm_dev", n)
            for _ in range(n if each else 1):
                e.wait_ge(norm_inv, c.of("norm_inv", 1, 1))
                c.add("norm_inv")
                e.activation(row, row, ACT.Sqrt).then_inc(norm_rstd, 1)
            if final:
                for j in range(n):
                    e.wait_ge(norm_out, c.of("norm_out", 1, j + 1))
                    final(e, j)
                c.add("norm_out", n)

        def x_tile(j):
            return x[:, j, :]

        def o_tile(j):
            return o[:, j, :]

        def affine(params, gain, shift):
            def final(e, j, src):
                e.activation(x[:, j, :], src(j), ACT.Identity, bias=params[:, shift + j:shift + j + 1],
                             scale=params[:, gain + j:gain + j + 1])
            return final

        def rope_pe(e, c, pairs, rot, tile):
            with c.loop(pairs, {"rope": 1}) as i:
                for b in range(2):
                    e.wait_ge(rot_free[b], c.of("rope", 1, 1))
                    e.matmul(ps[:, b, :], rot, big[:, tile(i, b), :], start=True, stop=True).then_inc(rot_full[b], 1)
                c.add("rope")

        def rope_dve(e, c, pairs, cos, sin, tile):
            with c.loop(pairs, {"rope": 1}) as i:
                for b in range(2):
                    e.wait_ge(rot_full[b], c.of("rope", 1, 1))
                    e.tensor_tensor(probs[:, b, 0:T], ps[:, b, :], sin, ALU.mult).then_inc(rot_free[b], 1)
                    e.tensor_tensor(big[:, tile(i, b), :], big[:, tile(i, b), :], cos, ALU.mult)
                e.drain()
                for b in range(2):
                    e.tensor_tensor(big[:, tile(i, b), :], big[:, tile(i, b), :], probs[:, b, 0:T], ALU.add)
                e.drain()
                c.add("rope")

        LEAD = 8
        SETS = 2

        def order(kind, ahead):
            alone = kind == "dil"
            done = 0
            for t in range(2 * QB):
                stop = t // QB * QB + QB if alone else 2 * QB
                if t == 0 or alone and t % QB == 0:
                    yield "values", t // QB
                elif t == QB - 2 and not alone:
                    if ahead == 1:
                        yield "head", done
                        done += 1
                    yield "values", 1
                while done < min(t + ahead + 1, stop):
                    yield "head", done
                    done += 1
                yield "tail", t

        def per_turn(kind):
            return {"steps": 2 * QB, "turns": t_turns(kind), "st0": STAGED[kind], "st1": STAGED[kind],
                    "kept": 2 * QB if kind == "sb" else 0}

        def width_of(kind):
            return P if kind == "diff" else 64

        def bank(t, s):
            return 3 * (t % 2) + s

        def offsets(segs):
            return [sum(P * g[4] for g in segs[:s]) for s in range(len(segs))]

        def v_at(kind, slot, kb):
            w = width_of(kind)
            return vtok[:, (slot * QB + kb) * w:(slot * QB + kb + 1) * w]

        def attend_sp(e, c, kind, pairs):
            with c.loop(pairs, per_turn(kind)) as i:
                for a in range(2):
                    e.wait_ge(scored, c.of("steps", 1, QB * a + (LEAD if kind == "dil" else QB)))
                    h = slice(64 * a, 64 * a + 64)
                    moves = []
                    if kind == "dil":
                        for br in range(3):
                            moves += [(st_q[0:64, br, :], big[h, i + (DIL_Q + 2 * br), :]),
                                      (st_k[0:64, br, :], big[h, i + (DIL_K + 2 * br), :]),
                                      (st_v[0:64, br, :], big[h, i + (DIL_V + 2 * br), :])]
                    elif kind == "diff":
                        moves = [(st_q[:, a, :], big[:, i * 2 + a, :]),
                                 (st_k[:, a, :], big[:, i * 2 + (HEADS1 + a), :]),
                                 (st_v[:, a, :], big[:, i * 2 + (2 * HEADS1 + a), :])]
                    elif kind == "mla":
                        moves = [(st_q[0:96, a, :], big[0:96, i * 2 + (MLA_Q + a), :]),
                                 (st_k[0:64, a, :], big[0:64, i * 2 + (MLA_KV + a), :]),
                                 (st_k[ROPE0:ROPE1, a, :], big[ROPE0:ROPE1, MISC, :]),
                                 (st_v[0:64, a, :], big[64:P, i * 2 + (MLA_KV + a), :])]
                    else:
                        q, k, v = (SB_Q, SB_K, SB_V) if kind == "sb" else (FOX_Q, FOX_K, FOX_V)
                        moves = [(st_q[0:64, a, :], big[h, i + q, :]), (st_k[0:64, a, :], big[h, i + k, :]),
                                 (st_v[0:64, a, :], big[h, i + v, :])]
                        if kind == "fox":
                            moves += [(st_q[64:65, a, :], big[0:1, i * 2 + (FOX_C + a), :]),
                                      (st_q[65:66, a, :], big[64:65, FOX_C, :]),
                                      (st_k[64:65, a, :], big[64:65, FOX_C, :]),
                                      (st_k[65:66, a, :], big[32:33, i * 2 + (FOX_C + a), :])]
                    assert len(moves) == STAGED[kind]
                    for dst, src in moves:
                        e.dma_start(dst, src).then_inc(staged[a], 16)
                c.add("steps", 2 * QB)
                c.add("turns", t_turns(kind))
                c.add("st0", STAGED[kind])
                c.add("st1", STAGED[kind])
                c.add("kept", 2 * QB if kind == "sb" else 0)

        def attend_pe(e, c, kind, pairs):
            plan, w = steps_of(kind), width_of(kind)
            with c.loop(pairs, per_turn(kind)) as i:
                for what, t in order(kind, 2):
                    if what == "values":
                        a = t
                        e.wait_ge(staged[a], c.of(f"st{a}", 16, 16 * STAGED[kind]))
                        c.add(f"st{a}", STAGED[kind])
                        for slot in range(3) if kind == "dil" else [a]:
                            e.wait_ge(t_free, c.of("turns", 1, 1))
                            settle(e)
                            for kb in range(QB):
                                m = e.transpose(ps[:, 6, kb * w:(kb + 1) * w], st_v[0:w, slot, kb * P:(kb + 1) * P],
                                                ident[0:w, 0:w])
                            m.then_inc(t_full, 1)
                            c.add("turns")
                    elif what == "head":
                        e.wait_ge(exp_done, c.of("steps", 1, t + 1))
                        segs = plan[t % QB]
                        for s, (slot, r0, r1, kb, n, _) in enumerate(segs):
                            slot = t // QB if slot is None else slot
                            m = e.matmul(ps[:, bank(t, s), 0:n * P], st_q[r0:r1, slot, (t % QB) * P:(t % QB + 1) * P],
                                         st_k[r0:r1, slot, kb * P:(kb + n) * P], start=True, stop=True)
                        m.then_inc(scored, 1)
                    else:
                        segs = plan[t % QB]
                        at, blocks = offsets(segs), blocks_of(kind, segs)
                        e.wait_ge(p_ready, c.of("steps", 1, t + 1))
                        for g in range(0, len(blocks), 4):
                            e.wait_ge(t_free, c.of("turns", 1, 1))
                            for j, (s, b) in enumerate(blocks[g:g + 4]):
                                m = e.transpose(ps[:, 6, j * P:(j + 1) * P],
                                                probs[:, t % 2, at[s] + b * P:at[s] + (b + 1) * P], ident)
                            m.then_inc(t_full, 1)
                            c.add("turns")
                        e.wait_ge(t_free, c.of("turns", 1, 1))
                        e.wait_ge(o_free, c.of("steps", 1, t + 1))
                        for j, (s, b) in enumerate(blocks):
                            slot = t // QB if segs[s][0] is None else segs[s][0]
                            m = e.matmul(ps[0:w, 7, 0:P], v_at(kind, slot, segs[s][3] + b), probs_t[:, j, :],
                                         start=j == 0, stop=j == len(blocks) - 1)
                        m.then_inc(o_full, 1)
                c.add("steps", 2 * QB)
                c.add("kept", 2 * QB if kind == "sb" else 0)

        def attend_act(e, c, kind, pairs):
            plan, w = steps_of(kind), width_of(kind)
            with c.loop(pairs, per_turn(kind)) as i:
                for what, t in order(kind, 1):
                    if what == "values":
                        e.wait_ge(o_full, c.of("steps", 1, SETS + (QB * t if kind == "dil" else 0)))
                        for slot in range(3) if kind == "dil" else [t]:
                            e.wait_ge(t_full, c.of("turns", 1, 1))
                            e.copy(vtok[:, slot * QB * w:(slot + 1) * QB * w], ps[:, 6, 0:QB * w]).then_inc(t_free, 1)
                            c.add("turns")
                    elif what == "head":
                        segs = plan[t % QB]
                        at = offsets(segs)
                        e.wait_ge(o_full, c.of("steps", 1, t + 1))
                        if kind == "sb":
                            n = segs[0][4] * P
                            z, p = ps[:, bank(t, 0), 0:n], probs[:, t % 2, 0:n]
                            e.wait_ge(scored, c.of("steps", 1, LEAD + t + 1))
                            e.activation(p, z, ACT.Abs)
                            e.drain()
                            e.activation(p, p, ACT.Exp, scale=-1.0)
                            e.drain()
                            e.activation(p, p, ACT.Ln, bias=1.0).then_inc(kept, 1)
                            e.wait_ge(max_ready, c.of("steps", 1, t + 1))
                            e.activation(p, p, ACT.Exp).then_inc(exp_done, 1)
                        else:
                            e.wait_ge(max_ready, c.of("steps", 1, t + 1))
                            for s, seg in enumerate(segs):
                                bias = s if kind == "diff" else 0
                                m = e.activation(probs[:, t % 2, at[s]:at[s] + seg[4] * P],
                                                 ps[:, bank(t, s), 0:seg[4] * P], ACT.Exp,
                                                 bias=stat[:, t % 2, bias:bias + 1],
                                                 accum_out=stat[:, t % 2, 8 + s:9 + s])
                            m.then_inc(exp_done, 1)
                    else:
                        e.wait_ge(o_full, c.of("steps", 1, SETS + t))
                        n = len(blocks_of(kind, plan[t % QB]))
                        for g in range(0, n, 4):
                            k = min(4, n - g)
                            e.wait_ge(t_full, c.of("turns", 1, 1))
                            e.copy(probs_t[:, g:g + k, :].rearrange("p a t -> p (a t)"), ps[:, 6, 0:k * P])\
                                .then_inc(t_free, 1)
                            c.add("turns")
                c.add("steps", 2 * QB)
                c.add("st0", STAGED[kind])
                c.add("st1", STAGED[kind])
                c.add("kept", 2 * QB if kind == "sb" else 0)

        def attend_dve(e, c, kind, pairs, o_first):
            plan, w = steps_of(kind), width_of(kind)

            def take_output(i, t):
                a, qs = t // QB, slice((t % QB) * P, (t % QB + 1) * P)
                dst = o[:, i * 2 + a, qs] if kind == "diff" else o[64 * a:64 * a + 64, i + o_first, qs]
                e.wait_ge(o_full, c.of("steps", 1, SETS + t + 1))
                e.tensor_copy(dst, ps[0:w, 7, 0:P]).then_inc(o_free, 1)

            with c.loop(pairs, per_turn(kind)) as i:
                for what, t in order(kind, 1):
                    if what == "values":
                        continue
                    segs = plan[t % QB]
                    at = offsets(segs)
                    st = stat[:, t % 2, :]
                    if what == "head" and kind == "sb":
                        n = segs[0][4] * P
                        z, p = ps[:, bank(t, 0), 0:n], probs[:, t % 2, 0:n]
                        e.wait_ge(kept, c.of("kept", 1, t + 1))
                        e.scalar_tensor_tensor(p, z, 0.0, p, ALU.max, ALU.add)
                        e.drain()
                        e.tensor_tensor(p[:, n - P:n], p[:, n - P:n], masks[:, M_KEEP:M_KEEP + P], ALU.mult)
                        e.drain()
                        e.tensor_tensor_scan(scan[:, 0:n][:, ::-1], p[:, ::-1], p[:, ::-1], 0.0, ALU.add, ALU.bypass)
                        e.drain()
                        e.tensor_tensor(p, z, scan[:, 0:n], ALU.subtract)
                        e.drain()
                        e.tensor_tensor(p[:, n - P:n], p[:, n - P:n], masks[:, M_STRICT:M_STRICT + P], ALU.add)\
                            .then_inc(max_ready, 1)
                    elif what == "head":
                        e.wait_ge(scored, c.of("steps", 1, LEAD + t + 1))
                        for s, seg in enumerate(segs):
                            n = seg[4] * P
                            m0 = 0 if kind == "dil" else n - P
                            z = ps[:, bank(t, s), m0:n]
                            e.tensor_tensor(z, z, masks[:, seg[5]:seg[5] + n - m0], ALU.add)
                        e.drain()
                        for s, seg in enumerate(segs):
                            col = 4 + s if kind == "dil" else s
                            m = e.tensor_reduce(st[:, col:col + 1], ps[:, bank(t, s), 0:seg[4] * P], AX.X, ALU.max,
                                                negate=kind != "dil")
                        if kind == "dil":
                            e.drain()
                            m = e.tensor_reduce(st[:, 0:1], st[:, 4:7], AX.X, ALU.max, negate=True)
                        m.then_inc(max_ready, 1)
                    else:
                        e.wait_ge(exp_done, c.of("steps", 1, SETS + t + 1))
                        if kind == "sb":
                            e.sem_inc(p_ready, 1)
                        elif kind == "diff":
                            n = segs[0][4] * P
                            p0, p1_ = probs[:, t % 2, 0:n], probs[:, t % 2, n:2 * n]
                            e.reciprocal(st[:, 12:14], st[:, 8:10])
                            e.drain()
                            e.tensor_scalar(p1_, p1_, st[:, 13:14], small[:, 4:5], ALU.mult, ALU.mult)
                            e.drain()
                            e.scalar_tensor_tensor(p0, p0, st[:, 12:13], p1_, ALU.mult, ALU.add).then_inc(p_ready, 1)
                        else:
                            n = sum(seg[4] for seg in segs) * P
                            if kind == "dil":
                                e.tensor_reduce(st[:, 11:12], st[:, 8:11], AX.X, ALU.add)
                                e.drain()
                            total = 11 if kind == "dil" else 8
                            e.reciprocal(st[:, 12:13], st[:, total:total + 1])
                            e.drain()
                            e.tensor_scalar(probs[:, t % 2, 0:n], probs[:, t % 2, 0:n], st[:, 12:13], None, ALU.mult)\
                                .then_inc(p_ready, 1)
                        if t:
                            take_output(i, t - 1)
                take_output(i, 2 * QB - 1)
                c.add("steps", 2 * QB)
                c.add("turns", t_turns(kind))
                c.add("st0", STAGED[kind])
                c.add("st1", STAGED[kind])
                c.add("kept", 2 * QB if kind == "sb" else 0)

        RG, RE, RPAD, RMAX, RIDX, RSEL, RV, RW = 0, 4, 24, 32, 40, 44, 48, 64

        def route_dve(e, c):
            iota = consts[:, C_IOTA:C_IOTA + EXPERTS]
            e.memset(route[:, :, RPAD:RPAD + 8], NEG)
            for q in range(QB):
                e.tensor_tensor(route[:, q, 0:20], ps[:, 0, 20 * q:20 * q + 20],
                                p2[:, COL2["router_b"]:COL2["router_b"] + 20], ALU.add)
            e.drain()
            e.tensor_copy(route[:, :, RPAD:RPAD + GROUPS], route[:, :, RG:RG + GROUPS])
            e.drain()
            for q in range(QB):
                e.max(route[:, q, RMAX:RMAX + 8], route[:, q, RPAD:RPAD + 8])
            e.drain()
            for q in range(QB):
                e.max_index(picks[:, q, :], route[:, q, RMAX:RMAX + 8], route[:, q, RPAD:RPAD + 8])
            for q in range(QB):
                e.tensor_scalar(route[:, q, RV:RV + GROUPS], route[:, q, RG:RG + GROUPS],
                                route[:, q, RMAX:RMAX + 1], None, ALU.subtract)
            e.drain()
            e.tensor_copy(route[:, :, RIDX:RIDX + 1], picks[:, :, 0:1]).then_inc(route_in, 1)
            e.drain()
            for q in range(QB):
                e.tensor_scalar(route[:, q, RSEL:RSEL + GROUPS], iota[:, 0:GROUPS], route[:, q, RIDX:RIDX + 1], None,
                                ALU.is_equal)
            e.drain()
            e.tensor_scalar(route[:, :, RSEL:RSEL + GROUPS], route[:, :, RSEL:RSEL + GROUPS], 1.0, -NEG,
                            ALU.subtract, ALU.mult)
            e.drain()
            for j in range(EXPERTS // GROUPS):
                view = route[:, :, RE + j:RE + EXPERTS:GROUPS]
                e.tensor_tensor(view, view, route[:, :, RSEL:RSEL + GROUPS], ALU.add)
            e.drain()
            for q in range(QB):
                e.max(route[:, q, RMAX:RMAX + 8], route[:, q, RE:RE + EXPERTS])
            e.drain()
            for q in range(QB):
                e.max_index(picks[:, q, :], route[:, q, RMAX:RMAX + 8], route[:, q, RE:RE + EXPERTS])
            e.tensor_tensor(route[:, :, RW:RW + 1], route[:, :, RMAX + 1:RMAX + 2], route[:, :, RMAX:RMAX + 1],
                            ALU.subtract).then_inc(route_in, 1)
            e.drain()
            e.tensor_copy(route[:, :, RIDX:RIDX + 2], picks[:, :, 0:2])
            e.wait_ge(route_exp, c.of("routes", 2, 2))
            c.add("routes")
            for q in range(QB):
                e.tensor_reduce(route[:, q, RW + 2:RW + 3], route[:, q, RV:RV + GROUPS], AX.X, ALU.add)
            e.tensor_scalar(route[:, :, RW + 3:RW + 4], route[:, :, RW:RW + 1], 1.0, None, ALU.add)
            e.drain()
            e.tensor_tensor(route[:, :, RW + 4:RW + 5], route[:, :, RW + 2:RW + 3], route[:, :, RW + 3:RW + 4], ALU.mult)
            e.drain()
            e.reciprocal(route[:, :, RW + 5:RW + 6], route[:, :, RW + 4:RW + 5])
            e.drain()
            e.tensor_tensor(route[:, :, RW + 6:RW + 7], route[:, :, RW + 5:RW + 6], route[:, :, RW:RW + 1], ALU.mult)
            e.drain()
            for q in range(QB):
                e.tensor_scalar(route[:, q, RE:RE + EXPERTS], iota, route[:, q, RIDX:RIDX + 1],
                                route[:, q, RW + 5:RW + 6], ALU.is_equal, ALU.mult)
                e.tensor_scalar(route[:, q, 72:72 + EXPERTS], iota, route[:, q, RIDX + 1:RIDX + 2],
                                route[:, q, RW + 6:RW + 7], ALU.is_equal, ALU.mult)
            e.drain()
            e.tensor_tensor(route[:, :, RE:RE + EXPERTS], route[:, :, RE:RE + EXPERTS], route[:, :, 72:72 + EXPERTS],
                            ALU.add)
            for j in range(DT):
                e.tensor_scalar(o[:, j, :], x[:, j, :], ALPHA, None, ALU.mult)
            e.drain()
            for k in range(EXPERTS):
                if k >= 2:
                    e.wait_ge(spread_full[k % 2], c.of("spread", 1, k // 2))
                for q in range(QB):
                    m = e.tensor_scalar(probs[:, k % 2, q * P:(q + 1) * P], ones, route[:, q, RE + k:RE + k + 1], None,
                                        ALU.mult)
                m.then_inc(spread_in, 1)
            c.add("spread", EXPERTS // 2)

        def route_act(e, c):
            e.wait_ge(route_in, c.of("routes", 2, 1))
            e.activation(route[:, :, RV:RV + GROUPS], route[:, :, RV:RV + GROUPS], ACT.Exp).then_inc(route_exp, 1)
            e.wait_ge(route_in, c.of("routes", 2, 2))
            e.activation(route[:, :, RW:RW + 1], route[:, :, RW:RW + 1], ACT.Exp).then_inc(route_exp, 1)
            c.add("routes")

        def route_pe(e):
            for q in range(QB):
                for k in range(DT):
                    e.matmul(ps[:, 0, 20 * q:20 * q + 20], x[:, k, q * P:(q + 1) * P],
                             p2[:, COL2["router"] + 20 * k:COL2["router"] + 20 * k + 20], start=k == 0, stop=k == DT - 1)

        def spread_pe(e, c):
            for k in range(EXPERTS):
                e.wait_ge(spread_in, c.of("spread", 2, k + 1))
                e.wait_ge(spread_free[k % 2], c.of("spread", 1, k // 2 + 1))
                for q in range(QB):
                    m = e.matmul(ps[:, 1 + k % 2, q * P:(q + 1) * P], probs[:, k % 2, q * P:(q + 1) * P], ident,
                                 start=True, stop=True)
                m.then_inc(spread_full[k % 2], 1)
            c.add("spread", EXPERTS // 2)

        def spread_act(e, c):
            for k in range(EXPERTS):
                e.wait_ge(spread_full[k % 2], c.of("spread", 1, k // 2 + 1))
                e.copy(big[:, k, :], ps[:, 1 + k % 2, :]).then_inc(spread_free[k % 2], 1)
            c.add("spread", EXPERTS // 2)

        block = es.enter_context(nc.Block())
        LAYER = {"group": W_IN2_GROUPS + 2 + 2 + 4 * EXPERTS, "phase": 14, "layer": 1, "rope": 6 + 3, "steps": 2 * 8 * 4,
                 "routes": 1, "spread": EXPERTS // 2, "norm_sum": 2, "norm_dev": 2 * DT, "norm_out": 2 * DT,
                 "norm_sq": 3 * DT + 3, "norm_inv": 4 + DT, "norm_var": 4 + DT, "norm_rstd": 4 + DT, "fox": 1,
                 "halves": 3 * DT, "hidden": EXPERTS * ET, "kept": 16, "turns": 2 * sum(t_turns(k) for k in ("dil", "mla", "fox", "sb")),
                 "st0": 2 * sum(STAGED[k] for k in ("dil", "mla", "fox", "sb")),
                 "st1": 2 * sum(STAGED[k] for k in ("dil", "mla", "fox", "sb"))}

        @block.sync
        def _(e):
            c = Counts(e)

            def load(dst, src, s):
                e.dma_start(dst, src).then_inc(s, 16)

            def feed_forward(layer):
                load_tiles(e, c, FT // 2, lambda i, b: a["w_up" if b % 2 else "w_gate"][layer, i * 2 + b // 2], DT * P)
                load_tiles(e, c, 4, lambda i, b: a["w_down"][layer, i * RING + b], SLOT)

            load(x[:, :, :], a["x"], const_in)
            load(p1[:, :], a["p1"], const_in)
            load(consts[:, :], a["consts"], const_in)
            load(masks[:, :], a["masks"], const_in)
            load(tabs[:, :, :], a["tabs"], const_in)
            load(gates_w, a["gates"], const_in)
            load_tiles(e, c, 4, lambda i, b: a["w_in"][i * RING + b], DT * P)
            load_tiles(e, c, 2, lambda i, b: a["w_out"][i * RING + b], DT * P)
            feed_forward(0)
            c.add("phase", 9)
            load_tiles(e, c, 6, lambda i, b: a["w_qkv"][i * RING + b], DT * P)
            c.add("phase", 2)
            phase_wait(e, c)
            attend_sp(e, c, "diff", HEADS1 // 2)
            load_tiles(e, c, 2, lambda i, b: a["w_out1"][i * RING + b], DT * P)
            feed_forward(1)
            c.add("phase", 7)
            with c.loop(LAYERS2, LAYER) as l:
                phase_wait(e, c)
                load(p2[:, :], a["p2"][l], layer_in)
                load_tiles(e, c, W_IN2_GROUPS, lambda i, b: a["w_in2"][l, i * RING + b], DT * P)
                c.add("phase", 2)
                phase_wait(e, c)
                attend_sp(e, c, "dil", 2)
                load_tiles(e, c, 1, lambda i, b: a["w_uq"][l, b], 2 * ROPE1)
                load_tiles(e, c, 1, lambda i, b: a["w_ukv"][l, b], P)
                c.add("phase", 2)
                phase_wait(e, c)
                for h in range(4):
                    load(big[0:1, FOX_C + h, :], probs[h:h + 1, 0, T:2 * T], fox_rows)
                    load(big[32:33, FOX_C + h, :], probs[h:h + 1, 1, T:2 * T], fox_rows)
                e.wait_ge(fox_rows, c.of("fox", 8 * 16, 8 * 16))
                settle(e)
                c.add("fox")
                c.add("phase", 2)
                phase_wait(e, c)
                attend_sp(e, c, "mla", 2)
                attend_sp(e, c, "fox", 2)
                attend_sp(e, c, "sb", 2)
                load_tiles(e, c, 2, lambda i, b: a["w_out2"][l, i * RING + b], DT * P)
                with c.loop(EXPERTS, {"group": 4}) as k:
                    for half in range(2):
                        for b in range(RING):
                            e.wait_ge(slot_split[b], c.of("group", 1, 1))
                            e.dma_start(ring[:, b, 0:DT * P], a["w3" if b % 2 else "w1"][l, k, 2 * half + b // 2])\
                                .then_inc(w_full[b], 16)
                        c.add("group")
                    for half in range(2):
                        for b in range(RING):
                            e.wait_ge(slot_split[b], c.of("group", 1, 1))
                            e.dma_start(ring[:, b, 0:ET * P], a["w2"][l, k, RING * half + b]).then_inc(w_full[b], 16)
                        c.add("group")
                c.add("phase", 8)
            phase_wait(e, c)
            load(out, x[:, :, :], out_done)
            e.wait_ge(out_done, 16)

        @block.tensor
        def _(e):
            c = Counts(e)
            e.sem_inc(scored, LEAD)
            for s in (*tile_done, *slot_split, *bank_free, *rot_free, *spread_free, t_free, o_free):
                e.sem_inc(s, 1)
            e.sem_inc(hid_done, 2)
            e.sem_inc(o_full, SETS)

            def ln(data):
                norm_pe(e, c, data, DT, ones, centred=True)
                phase(e, c)

            def feed_forward():
                halve_pe(e, c)
                mul_tiles(e, c, FT // 2, high)
                c.add("hidden", FT)
                phase(e, c)
                with c.loop(4, {"group": 1}) as i:
                    for b in range(RING):
                        e.wait_ge(slot_split[b], c.of("group", 1, 2))
                        if b % 2 == 0:
                            e.wait_ge(bank_free[b + 1], c.of("group", 1, 1))
                        for k in range(FT // 2):
                            kt = b % 2 * (FT // 2) + k
                            m = mul3(e, ps[:, b - b % 2, :], k, P, b, h_hi[:, kt, :], h_lo[:, kt, :],
                                     kt == 0, kt == FT - 1)
                        m.then_inc(tile_done[b], 1)
                    c.add("group")
                phase(e, c)
                ln(x_tile)

            e.wait_ge(const_in, 6 * 16)
            halve_pe(e, c)
            mul_tiles(e, c, 4, low)
            phase(e, c)
            phase(e, c)
            for j in range(AT):
                for g in range(2):
                    m = e.matmul(ps[:, 4 * g + j, :], gates_w[:, AT * g + j, :], big[:, 12 + j, :], start=True, stop=True)
                m.then_inc(sg_ready, 1)
            phase(e, c)
            norm_pe(e, c, lambda j: big[:, 8 + j, :], AT, ones, centred=True)
            phase(e, c)
            halve_pe(e, c)
            mul_tiles(e, c, 2, low)
            phase(e, c)
            ln(x_tile)
            feed_forward()
            halve_pe(e, c)
            mul_tiles(e, c, 6, high)
            phase(e, c)
            rope_pe(e, c, HEADS1, consts[:, C_ROT:C_ROT + P], lambda i, b: i * 2 + b)
            phase(e, c)
            attend_pe(e, c, "diff", HEADS1 // 2)
            phase(e, c)
            norm_pe(e, c, o_tile, HEADS1, ones, each=True)
            phase(e, c)
            halve_pe(e, c)
            mul_tiles(e, c, 2, low)
            phase(e, c)
            ln(x_tile)
            feed_forward()
            with c.loop(LAYERS2, LAYER) as l:
                e.wait_ge(layer_in, c.of("layer", 16, 16))
                settle(e)
                c.add("layer")
                halve_pe(e, c)
                mul_tiles(e, c, W_IN2_GROUPS, high)
                phase(e, c)
                for first in (DIL_Q, DIL_K):
                    rope_pe(e, c, 3, consts[:, C_ROT:C_ROT + P], lambda i, b: i * 2 + (first + b))
                phase(e, c)
                attend_pe(e, c, "dil", 2)
                phase(e, c)
                norm_pe(e, c, lambda j: big[:, CQ + j, :], 2, ones)
                norm_pe(e, c, lambda j: big[:, CKV + j, :], 1, ones)
                phase(e, c)
                for kt, first, rows in ((2, CQ, ROPE1), (1, CKV, P)):
                    for b in range(RING):
                        e.wait_ge(w_full[b], c.of("group", 16, 16))
                        e.wait_ge(bank_free[b], c.of("group", 1, 1))
                        for k in range(kt):
                            m = e.matmul(ps[0:rows, b, :], ring[:, b, k * rows:(k + 1) * rows], big[:, first + k, :],
                                         start=k == 0, stop=k == kt - 1)
                        m.then_inc(tile_done[b], 1)
                    c.add("group")
                phase(e, c)
                rope_pe(e, c, 2, consts[:, C_ROTM:C_ROTM + P], lambda i, b: i * 2 + (MLA_Q + b))
                rope_pe(e, c, 1, consts[:, C_ROTM:C_ROTM + P], lambda i, b: MISC if b == 0 else MLA_Q + 4)
                phase(e, c)
                attend_pe(e, c, "mla", 2)
                attend_pe(e, c, "fox", 2)
                attend_pe(e, c, "sb", 2)
                phase(e, c)
                norm_pe(e, c, o_tile, DT, half1, each=True)
                phase(e, c)
                halve_pe(e, c)
                mul_tiles(e, c, 2, low)
                phase(e, c)
                ln(x_tile)
                route_pe(e)
                phase(e, c)
                spread_pe(e, c)
                phase(e, c)
                halve_pe(e, c)
                with c.loop(EXPERTS, {"group": 4, "hidden": ET}) as k:
                    for half in range(2):
                        for b in range(RING):
                            e.wait_ge(slot_split[b], c.of("group", 1, 2))
                            e.wait_ge(bank_free[b], c.of("group", 1, 1))
                            for kt in range(DT):
                                m = mul3(e, ps[:, b, :], kt, P, b, low[0][:, kt, :], low[1][:, kt, :],
                                         kt == 0, kt == DT - 1)
                            m.then_inc(tile_done[b], 1)
                        c.add("group")
                    e.wait_ge(hid_done, c.of("hidden", 1, 2 + ET))
                    c.add("hidden", ET)
                    for half in range(2):
                        for b in range(RING):
                            e.wait_ge(slot_split[b], c.of("group", 1, 2))
                            e.wait_ge(bank_free[b], c.of("group", 1, 1))
                            for kt in range(ET):
                                m = mul3(e, ps[:, b, :], kt, P, b, eh_hi[:, kt, :], eh_lo[:, kt, :],
                                         kt == 0, kt == ET - 1)
                            m.then_inc(tile_done[b], 1)
                        c.add("group")
                phase(e, c)
                ln(o_tile)

        @block.scalar
        def _(e):
            c = Counts(e)
            e.sem_inc(exp_done, SETS)

            def ln(data, params, gain, shift):
                f = affine(params, gain, shift)
                norm_act(e, c, data, DT, centred=True, final=lambda e, j: f(e, j, data))
                phase(e, c)

            def col(name, j=0):
                return p1[:, COL1[name] + j:COL1[name] + j + 1]

            def copies(dst, scale=1.0):
                def take(i, b):
                    if b % 2 == 0:
                        return e.activation(dst(i, b), ps[:, b, :], ACT.Copy, scale=scale)
                return take

            def nothing(i, b):
                return None

            def take_one(b, dst, scale=1.0):
                e.wait_ge(tile_done[b], c.of("group", 1, 2))
                e.activation(dst, ps[0:dst.shape[0], b, :], ACT.Copy, scale=scale).then_inc(bank_free[b], 1)

            def out_product(src):
                halve_act(e, c, low, src)
                take_tiles(e, c, 2, split_act, DT * P, nothing)
                phase(e, c)

            def feed_forward(layer):
                halve_act(e, c, high, x_tile)

                def take(i, b):
                    if b % 2 == 0:
                        return silu_act(e, c, b, b // 2)

                hidden_tiles(e, c, split_act, take)
                phase(e, c)
                take_tiles(e, c, 4, split_act, SLOT, nothing)
                phase(e, c)
                ln(x_tile, p1, COL1[f"fg{layer}"], COL1[f"fb{layer}"])

            e.wait_ge(const_in, 6 * 16)
            e.activation(small[:, 8:12], p1[:, COL1["lam"]:COL1["lam"] + AT], ACT.Abs)
            e.drain()
            e.activation(small[:, 12:16], small[:, 8:12], ACT.Exp, scale=-1.0)
            e.drain()
            e.activation(small[:, 16:20], small[:, 12:16], ACT.Ln, bias=1.0)
            halve_act(e, c, low, x_tile)

            def gates(j, b):
                if b == 0:
                    return e.activation(big[:, j, :], ps[:, 0, :], ACT.Sigmoid, bias=col("b_in", 4 * j))
                if b == 2:
                    return e.activation(big[:, 4 + j, :], ps[:, 2, :], ACT.Gelu_apprx_tanh, bias=col("b_in", 4 * j + 2))

            take_tiles(e, c, 4, split_act, DT * P, gates, loop=False)
            phase(e, c)
            phase(e, c)
            e.activation(small[:, 20:22], small[:, 2:4], ACT.Exp)
            for j in range(AT):
                e.wait_ge(sg_ready, j + 1)
                e.activation(big[:, 16 + j, :], ps[:, j, :], ACT.Sigmoid, bias=col("b_a", j))
                e.activation(big[:, 20 + j, :], ps[:, 4 + j, :], ACT.Sigmoid, bias=col("b_x", j))
            e.drain()
            for j in range(AT):
                e.activation(big[:, 16 + j, :], big[:, 16 + j, :], ACT.Tanh, scale=small[:, 24 + j:25 + j])
            e.drain()
            e.activation(big[:, 24:28, :], big[:, 16:20, :], ACT.Sqrt)
            phase(e, c)
            norm_act(e, c, lambda j: big[:, 8 + j, :], AT, centred=True,
                     final=lambda e, j: e.activation(big[:, 8 + j, :], big[:, 8 + j, :], ACT.Silu, bias=col("cn_b", j),
                                                     scale=col("cn_g", j)))
            phase(e, c)
            out_product(lambda j: big[:, 8 + j, :])
            ln(x_tile, p1, COL1["mg0"], COL1["mb0"])
            feed_forward(0)
            halve_act(e, c, high, x_tile)
            take_tiles(e, c, 2, split_act, DT * P, copies(lambda i, b: big[:, i * RING + b, :], 0.125), end=False)
            take_tiles(e, c, 4, split_act, DT * P, copies(lambda i, b: big[:, i * RING + (8 + b), :]), start=False)
            phase(e, c)
            c.add("rope", HEADS1)
            phase(e, c)
            attend_act(e, c, "diff", HEADS1 // 2)
            phase(e, c)
            norm_act(e, c, o_tile, HEADS1, each=True)
            phase(e, c)
            out_product(o_tile)
            ln(x_tile, p1, COL1["mg1"], COL1["mb1"])
            feed_forward(1)
            with c.loop(LAYERS2, LAYER) as l:
                e.wait_ge(layer_in, c.of("layer", 16, 16))
                settle(e)
                c.add("layer")
                halve_act(e, c, high, x_tile)
                w = DT * P
                take_tiles(e, c, 2, split_act, w, copies(lambda i, b: big[:, i * RING + b, :], 0.125), end=False)
                take_tiles(e, c, 1, split_act, w, lambda i, b: copies(
                    lambda i, b: big[:, FOX_Q + b, :], 1.0 if b == 2 else 0.125)(i, b), start=False, end=False)
                take_tiles(e, c, 5, split_act, w, copies(lambda i, b: big[:, i * RING + (DIL_K + b), :]),
                           start=False, end=False)
                take_tiles(e, c, 1, split_act, w, copies(lambda i, b: big[:, CKV, :] if b == 0 else probs[:, 0, 0:T]),
                           start=False)
                phase(e, c)
                phase(e, c)
                attend_act(e, c, "dil", 2)
                phase(e, c)
                norm_act(e, c, lambda j: big[:, CQ + j, :], 2)
                norm_act(e, c, lambda j: big[:, CKV + j, :], 1)
                f, g = probs[0:4, 0, 0:T], probs[0:4, 1, 0:T]
                e.activation(f, big[0:4, MISC, :], ACT.Identity, bias=p2[0:4, COL2["b_f"]:COL2["b_f"] + 1])
                e.drain()
                e.activation(g, f, ACT.Abs)
                e.drain()
                e.activation(g, g, ACT.Exp, scale=-1.0)
                e.drain()
                e.activation(g, g, ACT.Ln, bias=1.0).then_inc(kept_gate, 1)
                phase(e, c)
                for b in range(RING):
                    take_one(b, big[0:ROPE1, MLA_Q + b, :], float(ROPE1) ** -0.5)
                c.add("group")
                for b in (0, 2):
                    take_one(b, big[:, MLA_KV + b, :])
                c.add("group")
                for b in range(RING):
                    e.sem_inc(hi_done[b], 2)
                phase(e, c)
                phase(e, c)
                attend_act(e, c, "mla", 2)
                attend_act(e, c, "fox", 2)
                attend_act(e, c, "sb", 2)
                phase(e, c)
                norm_act(e, c, o_tile, DT, each=True)
                phase(e, c)
                out_product(o_tile)
                ln(x_tile, p2, COL2["ln1_g"], COL2["ln1_b"])
                phase(e, c)
                route_act(e, c)
                spread_act(e, c)
                phase(e, c)
                halve_act(e, c, low, x_tile)

                def take(k, g, b):
                    if g < 2 and b % 2 == 0:
                        return silu_act(e, c, b, b // 2)

                expert_tiles(e, c, split_act, take)
                phase(e, c)
                ln(o_tile, p2, COL2["ln2_g"], COL2["ln2_b"])

        @block.vector
        def _(e):
            c = Counts(e)

            def ln(data):
                norm_dve(e, c, data, DT, D, LN_EPS, centred=True)
                phase(e, c)

            def col(name, j=0):
                return p1[:, COL1[name] + j:COL1[name] + j + 1]

            def out_product(src):
                def take(i, b):
                    xt = x[:, i * RING + b, :]
                    return e.scalar_tensor_tensor(xt, xt, ALPHA, ps[:, b, :], ALU.mult, ALU.add)

                halve_dve(e, c, low, src)
                take_tiles(e, c, 2, split_dve, DT * P, take)
                phase(e, c)

            def feed_forward():
                def hidden(i, b):
                    if b % 2:
                        j = i * 2 + b // 2
                        hidden_dve(e, c, b, b // 2, h_hi[:, j, :], h_lo[:, j, :])

                def take(i, b):
                    if b % 2:
                        xt = x[:, i * 2 + b // 2, :]
                        e.sem_inc(bank_free[b - 1], 1)
                        return e.scalar_tensor_tensor(xt, xt, ALPHA, ps[:, b - 1, :], ALU.mult, ALU.add)

                halve_dve(e, c, high, x_tile)
                hidden_tiles(e, c, split_dve, hidden)
                phase(e, c)
                take_tiles(e, c, 4, split_dve, SLOT, take)
                phase(e, c)
                ln(x_tile)

            def copies(dst, scale=1.0):
                def take(i, b):
                    if b % 2:
                        return e.tensor_scalar(dst(i, b), ps[:, b, :], scale, None, ALU.mult)
                return take

            def take_one(b, dst, scale=1.0):
                e.wait_ge(tile_done[b], c.of("group", 1, 2))
                e.tensor_scalar(dst, ps[:, b, :], scale, None, ALU.mult).then_inc(bank_free[b], 1)

            def taps(src, width, weights, bias, dst):
                for j in range(AT):
                    e.tensor_scalar(dst(j), src(j, 0), col(weights, j), col(bias, j), ALU.mult, ALU.add)
                for k in range(1, width):
                    e.drain()
                    for j in range(AT):
                        e.scalar_tensor_tensor(dst(j), src(j, k), col(weights, AT * k + j), dst(j), ALU.mult, ALU.add)

            e.wait_ge(const_in, 6 * 16)
            e.memset(u_buf[:, :, 0:CONV - 1], 0.0)
            e.memset(rec[:, :, 0:LCONV - 1], 0.0)
            halve_dve(e, c, low, x_tile)

            def mixer_in(j, b):
                if b == 1:
                    e.wait_ge(bank_free[0], c.of("group", 1, 2))
                    return e.scalar_tensor_tensor(u_buf[:, j, CONV - 1:CONV - 1 + T], ps[:, 1, :],
                                                  col("b_in", 4 * j + 1), big[:, j, :], ALU.add, ALU.mult)
                if b == 3:
                    return e.tensor_scalar(rec[:, j, LCONV - 1:LCONV - 1 + T], ps[:, 3, :], col("b_in", 4 * j + 3),
                                           None, ALU.add)

            take_tiles(e, c, 4, split_dve, DT * P, mixer_in, loop=False)
            phase(e, c)
            taps(lambda j, k: rec[:, j, k:k + T], LCONV, "lconv_w", "lconv_b", lambda j: big[:, 12 + j, :])
            e.tensor_scalar(small[:, 24:28], p1[:, COL1["lam"]:COL1["lam"] + AT], -1.0, 0.0, ALU.mult, ALU.max)
            lamv = p1[:, COL1["lamv"]:COL1["lamv"] + 256].rearrange("p (a b d) -> p a b d", a=2, b=2)
            dots = scan[:, 0:P].rearrange("p (a d) -> p a d", a=2)
            e.tensor_tensor(dots, lamv[:, :, 0, :], lamv[:, :, 1, :], ALU.mult)
            e.tensor_scalar(small[:, 5:6], col("subln"), 1.0 - LAMBDA_INIT, None, ALU.mult)
            e.drain()
            e.tensor_tensor(small[:, 24:28], small[:, 24:28], small[:, 16:20], ALU.add)
            e.tensor_reduce(small[:, 2:4], dots, AX.X, ALU.add)
            e.drain()
            e.tensor_scalar(small[:, 24:28], small[:, 24:28], 4.0, None, ALU.mult)
            phase(e, c)
            taps(lambda j, k: u_buf[:, j, k:k + T], CONV, "conv_w", "conv_b", lambda j: big[:, 8 + j, :])
            phase(e, c)
            e.tensor_tensor(small[:, 4:5], small[:, 21:22], small[:, 20:21], ALU.subtract)
            e.drain()
            e.tensor_scalar(small[:, 4:5], small[:, 4:5], LAMBDA_INIT, None, ALU.subtract)
            norm_dve(e, c, lambda j: big[:, 8 + j, :], AT, AT * P, LN_EPS, centred=True)
            h, gi, root, den = big[:, 16:20, :], big[:, 20:24, :], big[:, 24:28, :], big[:, 28:32, :]
            e.tensor_scalar(den, h, 1.0, None, ALU.add)
            e.tensor_tensor(gi, gi, big[:, 12:16, :], ALU.mult)
            e.drain()
            e.reciprocal(den, den)
            e.tensor_scalar(h, h, -1.0, 1.0, ALU.mult, ALU.add)
            e.tensor_tensor(gi, gi, root, ALU.mult)
            e.drain()
            e.tensor_tensor(h, h, den, ALU.mult)
            for j in range(AT):
                e.scalar_tensor_tensor(gi[:, j, :], gi[:, j, :], 2.0, den[:, j, :], ALU.mult, ALU.mult)
            e.drain()
            for j in range(AT):
                e.tensor_tensor_scan(root[:, j, :], h[:, j, :], gi[:, j, :], 0.0, ALU.mult, ALU.add)
            e.drain()
            e.tensor_tensor(big[:, 12:16, :], root, big[:, 4:8, :], ALU.mult)
            phase(e, c)
            out_product(lambda j: big[:, 8 + j, :])
            ln(x_tile)
            feed_forward()
            halve_dve(e, c, high, x_tile)
            take_tiles(e, c, 2, split_dve, DT * P, copies(lambda i, b: big[:, i * RING + b, :], 0.125), end=False)
            take_tiles(e, c, 4, split_dve, DT * P, copies(lambda i, b: big[:, i * RING + (8 + b), :]), start=False)
            phase(e, c)
            rope_dve(e, c, HEADS1, tabs[:, 0, :], tabs[:, 1, :], lambda i, b: i * 2 + b)
            phase(e, c)
            attend_dve(e, c, "diff", HEADS1 // 2, 0)
            phase(e, c)
            norm_dve(e, c, o_tile, HEADS1, P, LN_EPS, each=True, scaled=lambda j: small[:, 5:6])
            phase(e, c)
            out_product(o_tile)
            ln(x_tile)
            feed_forward()
            with c.loop(LAYERS2, LAYER) as l:
                e.wait_ge(layer_in, c.of("layer", 16, 16))
                settle(e)
                c.add("layer")
                halve_dve(e, c, high, x_tile)
                w = DT * P
                take_tiles(e, c, 2, split_dve, w, copies(lambda i, b: big[:, i * RING + b, :], 0.125), end=False)
                take_tiles(e, c, 1, split_dve, w, lambda i, b: copies(
                    lambda i, b: big[:, FOX_Q + b, :], 1.0 if b == 3 else 0.125)(i, b), start=False, end=False)
                take_tiles(e, c, 5, split_dve, w, copies(lambda i, b: big[:, i * RING + (DIL_K + b), :]),
                           start=False, end=False)
                take_tiles(e, c, 1, split_dve, w, copies(lambda i, b: big[:, MISC, :] if b == 1 else probs[:, 1, 0:T]),
                           start=False)
                phase(e, c)
                for first in (DIL_Q, DIL_K):
                    rope_dve(e, c, 3, tabs[:, 0, :], tabs[:, 1, :], lambda i, b: i * 2 + (first + b))
                phase(e, c)
                attend_dve(e, c, "dil", 2, 6)
                phase(e, c)
                norm_dve(e, c, lambda j: big[:, CQ + j, :], 2, 2 * P, RMS_EPS,
                         scaled=lambda j: p2[:, COL2["g_cq"] + j:COL2["g_cq"] + j + 1])
                e.drain()
                norm_dve(e, c, lambda j: big[:, CKV + j, :], 1, P, RMS_EPS,
                         scaled=lambda j: p2[:, COL2["g_ckv"]:COL2["g_ckv"] + 1])
                e.wait_ge(kept_gate, c.of("fox", 1, 1))
                c.add("fox")
                f, g = probs[0:4, 0, :], probs[0:4, 1, :]
                e.scalar_tensor_tensor(f[:, 0:T], f[:, 0:T], 0.0, g[:, 0:T], ALU.min, ALU.subtract)
                e.drain()
                e.tensor_tensor_scan(f[:, T:2 * T], f[:, 0:T], f[:, 0:T], 0.0, ALU.add, ALU.bypass)
                e.memset(big[64:65, FOX_C, :], 1.0)
                e.drain()
                e.tensor_scalar(g[:, T:2 * T], f[:, T:2 * T], -1.0, None, ALU.mult)
                phase(e, c)
                for b in range(RING):
                    e.wait_ge(tile_done[b], c.of("group", 1, 2))
                    e.sem_inc(slot_split[b], 1)
                c.add("group")
                for b in range(RING):
                    if b % 2:
                        take_one(b, big[:, MLA_KV + b, :])
                    else:
                        e.wait_ge(tile_done[b], c.of("group", 1, 2))
                    e.sem_inc(slot_split[b], 1)
                c.add("group")
                phase(e, c)
                cosm, sinm = tabs[:, 2, :], tabs[:, 3, :]
                rope_dve(e, c, 2, cosm, sinm, lambda i, b: i * 2 + (MLA_Q + b))
                rope_dve(e, c, 1, cosm, sinm, lambda i, b: MISC if b == 0 else MLA_Q + 4)
                phase(e, c)
                attend_dve(e, c, "mla", 2, 4)
                attend_dve(e, c, "fox", 2, 2)
                attend_dve(e, c, "sb", 2, 0)
                phase(e, c)
                norm_dve(e, c, o_tile, DT, 64, RMS_EPS, each=True,
                         scaled=lambda j: p2[:, COL2["g_head"] + j:COL2["g_head"] + j + 1])
                phase(e, c)
                out_product(o_tile)
                ln(x_tile)
                phase(e, c)
                route_dve(e, c)
                phase(e, c)
                halve_dve(e, c, low, x_tile)

                def take(k, g, b):
                    if g >= 2:
                        y = o[:, RING * (g - 2) + b, :]
                        return e.tensor_tensor(y, y, ps[:, b, :], ALU.add)
                    if b % 2:
                        j = 2 * g + b // 2
                        hidden_dve(e, c, b, b // 2, eh_hi[:, j, :], eh_lo[:, j, :], big[:, k, :])

                expert_tiles(e, c, split_dve, take)
                phase(e, c)
                ln(o_tile)


def rotation(rows):
    r = np.zeros((P, P), np.float32)
    for start, width in rows:
        half = width // 2
        for d in range(half):
            r[start + half + d, start + d] = -1.0
            r[start + d, start + half + d] = 1.0
    return r


def constants():
    q, k = np.arange(P)[:, None], np.arange(P)[None, :]
    q4, k4 = q + T - P, np.arange(T)[None, :]
    masks = np.zeros((P, M_COLS), np.float32)
    masks[:, M_BAND:M_BAND + P] = np.where(k >= q, 0, NEG)
    masks[:, M_TRI:M_TRI + P] = np.where(k <= q, 0, NEG)
    masks[:, M_MOD4:M_MOD4 + T] = np.where((k4 <= q4) & ((q4 - k4) % 4 == 0), 0, NEG)
    masks[:, M_MOD16:M_MOD16 + T] = np.where((k4 <= q4) & ((q4 - k4) % 16 == 0), 0, NEG)
    masks[:, M_CHUNK:M_CHUNK + P] = np.where(k // 64 <= q // 64, 0, NEG)
    masks[:, M_STRICT:M_STRICT + P] = np.where(k < q, 0, NEG)
    masks[:, M_KEEP:M_KEEP + P] = np.where(k < q, 1, 0)
    consts = np.zeros((P, C_COLS), np.float32)
    consts[:, C_ID:C_ID + P] = np.eye(P)
    consts[:, C_ONE:C_ONE + P] = 1.0
    consts[:, C_HALF:C_HALF + P] = q // 64 == k // 64
    consts[:, C_ROT:C_ROT + P] = rotation([(0, 64), (64, 64)])
    consts[:, C_ROTM:C_ROTM + P] = rotation([(ROPE0, ROPE1 - ROPE0)])
    consts[:, C_IOTA:C_IOTA + EXPERTS] = np.arange(EXPERTS)
    tabs = np.zeros((P, 4, T), np.float32)
    tabs[:, 2, :] = 1.0

    def angles(half):
        inv = np.float32(10000.0) ** (-np.arange(half, dtype=np.float32) / np.float32(half))
        ang = np.arange(T, dtype=np.float32)[None, :] * inv.astype(np.float32)[:, None]
        return np.cos(ang), np.sin(ang)

    cos, sin = angles(32)
    tabs[:, 0, :], tabs[:, 1, :] = np.tile(cos, (4, 1)), np.tile(sin, (4, 1))
    cos, sin = angles(16)
    tabs[ROPE0:ROPE1, 2, :], tabs[ROPE0:ROPE1, 3, :] = np.tile(cos, (2, 1)), np.tile(sin, (2, 1))
    return masks, consts, tabs


def by_tile(w, cols=P):
    *lead, k, n = w.shape
    m = len(lead)
    w = w.reshape(*lead, k // P, P, n // cols, cols)
    w = np.transpose(w, (*range(m), m + 2, m + 1, m, m + 3))
    return np.ascontiguousarray(w).reshape(*lead, n // cols, P, (k // P) * cols)


def by_half(w):
    *lead, tiles, p, n = w.shape
    w = np.moveaxis(w.reshape(*lead, tiles, p, 2, n // 2), -2, -3)
    return np.ascontiguousarray(w).reshape(*lead, 2 * tiles, p, n // 2)


def by_column(v):
    return v.reshape(-1, P).T


def pack(parts):
    return np.ascontiguousarray(np.concatenate(parts, axis=1))


def lay_out(i):
    g = {k: np.asarray(v) for k, v in i.items()}
    masks, consts, tabs = constants()
    order = [b * AT + j for j in range(AT) for b in (1, 0, 2, 3)]
    w_in = by_tile(g["even_w_in"][0])[order]
    b_in = g["even_b_in"][0].reshape(16, P)[order].reshape(-1)
    gates = np.zeros((P, 2 * AT, P), np.float32)
    for n, name in enumerate(("even_w_a", "even_w_x")):
        for j in range(AT):
            for s in range(2):
                gates[64 * s:64 * s + 64, AT * n + j, 64 * s:64 * s + 64] = g[name][0, 2 * j + s]
    lamv = np.concatenate([g[f"odd_lambda_{v}"][0] for v in ("q1", "k1", "q2", "k2")])
    p1 = pack([by_column(b_in), by_column(g["even_conv_w"][0]), by_column(g["even_conv_b"][0]),
               by_column(g["even_cnorm_g"][0]), by_column(g["even_cnorm_b"][0]), by_column(g["even_lru_conv_w"][0]),
               by_column(g["even_lru_conv_b"][0]), by_column(g["even_b_a"][0]), by_column(g["even_b_x"][0]),
               by_column(g["even_lru_lambda"][0]), by_column(g["odd_subln_g"][0]),
               np.broadcast_to(lamv[None, :], (P, 256))]
              + [by_column(g[f"{w}_ln_{v}"][l]) for l in range(DEPTH) for w in ("mix", "ffn") for v in ("g", "b")])
    w2 = g["w_in_2"]
    at = {"sb": 0, "fox": 768, "f": 1536, "cq": 1540, "ckv": 1796, "kr": 1924, "dil": 1956}
    misc = np.zeros((LAYERS2, D, 3 * P), np.float32)
    misc[:, :, 0:4] = w2[:, :, at["f"]:at["f"] + 4]
    misc[:, :, ROPE0:ROPE1] = w2[:, :, at["kr"]:at["kr"] + 32]

    def cut(name, first, n):
        return w2[:, :, at[name] + first:at[name] + first + n]

    w_in2 = np.concatenate([cut("dil", 0, 768), cut("sb", 0, 256), cut("fox", 0, 256), cut("cq", 0, 256),
                            cut("dil", 768, 768), cut("sb", 256, 256), cut("fox", 256, 256), cut("dil", 1536, 768),
                            cut("sb", 512, 256), cut("fox", 512, 256), cut("ckv", 0, 128), misc], axis=2)
    b_f = np.zeros((LAYERS2, P, 1), np.float32)
    b_f[:, 0:4, 0] = g["b_forget_2"]
    router = np.concatenate([g["w_group_2"], g["w_expert_2"]], axis=2)
    router_b = np.concatenate([g["b_group_2"], g["b_expert_2"]], axis=1)
    p2 = np.stack([pack([by_column(g["g_cq_2"][l]), by_column(g["g_ckv_2"][l]), by_column(g["g_head_2"][l]),
                         by_column(g["ln1_g_2"][l]), by_column(g["ln1_b_2"][l]), by_column(g["ln2_g_2"][l]),
                         by_column(g["ln2_b_2"][l]), b_f[l],
                         router[l].reshape(DT, P, 20).transpose(1, 0, 2).reshape(P, DT * 20),
                         np.broadcast_to(router_b[l][None, :], (P, 20))]) for l in range(LAYERS2)])
    return {
        "x": np.ascontiguousarray(g["x"][0].T.reshape(DT, P, T).transpose(1, 0, 2)),
        "p1": p1, "p2": p2, "consts": consts, "masks": masks, "tabs": tabs, "gates": gates,
        "w_in": np.ascontiguousarray(w_in), "w_out": by_tile(g["even_w_out"][0]),
        "w_gate": by_tile(g["ffn_w_gate"]), "w_up": by_tile(g["ffn_w_up"]), "w_down": by_half(by_tile(g["ffn_w_down"])),
        "w_qkv": by_tile(g["odd_w_qkv"][0]), "w_out1": by_tile(g["odd_w_out"][0]),
        "w_in2": by_tile(w_in2), "w_uq": by_tile(g["w_uq_2"], ROPE1), "w_ukv": by_tile(g["w_ukv_2"]),
        "w_out2": by_tile(g["w_out_2"]), "w1": by_tile(g["w1_2"]), "w3": by_tile(g["w3_2"]), "w2": by_tile(g["w2_2"]),
    }


def kernel(**inputs):
    import concourse.bacc as bacc
    from concourse.bass_utils import run_bass_kernel_spmd

    nc = bacc.Bacc("TRN2", target_bir_lowering=False, num_devices=1)
    arrays = lay_out(inputs)
    a = {name: nc.dram_tensor(name, v.shape, F32, kind="ExternalInput").ap() for name, v in arrays.items()}
    out = nc.dram_tensor("out", (P, DT, T), F32, kind="ExternalOutput").ap()
    build(nc, a, out)
    r = run_bass_kernel_spmd(nc, [arrays], core_ids=[0])
    y = np.asarray(r.results[0]["out"])
    return np.ascontiguousarray(y.transpose(1, 0, 2).reshape(D, T).T).reshape(1, T, D)
```
